# Optimizing a Trainium2 kernel written in Bass

```python
import jax, jax.numpy as jnp
from jax import lax
import numpy as np

D_MODEL = 1024
BATCH = 1
SEQ = 1024
DEPTH = 1

HG_WIDTH = D_MODEL // 2
NSA_WIDTH = D_MODEL - HG_WIDTH
HG_EXPAND = 128
HG_HEADS = HG_WIDTH // HG_EXPAND
HG_DK = HG_EXPAND
HG_DV = HG_WIDTH // HG_HEADS
HG_CHUNK = 64
NSA_HEAD_DIM = 64
NSA_HEADS = NSA_WIDTH // NSA_HEAD_DIM
NSA_KV_GROUPS = 2
NSA_GROUP_SIZE = NSA_HEADS // NSA_KV_GROUPS
CMP_BLOCK = 32
CMP_STRIDE = 16
CMP_HIDDEN = 256
SLC_BLOCK = 64
SLC_TOPN = 16
WINDOW = 512
Q_BLOCK = 128
NEG = -1e30
FORCE = 1e4
D_FF = -(-8 * D_MODEL // (3 * 256)) * 256
ALPHA = (2.0 * DEPTH) ** 0.25
BETA = (8.0 * DEPTH) ** -0.25
LN_EPS = 1e-5
RMS_EPS = 1e-6
KV_W = NSA_KV_GROUPS * NSA_HEAD_DIM
IN_SIZES = [HG_WIDTH] * 4 + [NSA_WIDTH] + [KV_W] * 6 + [3 * NSA_HEADS]
IN_COLS = sum(IN_SIZES)

kernel_name = "hybrid_hgrn2_nsa_deepnorm_adaln_block"

def layer_norm(x, g, b):
    xf = x.astype(jnp.float32)
    mu = jnp.mean(xf, -1, keepdims=True)
    var = jnp.mean(jnp.square(xf - mu), -1, keepdims=True)
    return ((xf - mu) * lax.rsqrt(var + LN_EPS) * g + b).astype(x.dtype)

def alibi_slopes():
    s = 2.0 ** (-8.0 * (np.arange(NSA_HEADS) + 1) / NSA_HEADS)
    return jnp.asarray(s, jnp.float32).reshape(NSA_KV_GROUPS, NSA_GROUP_SIZE)

def hgrn2_mixer(q, f_logit, inp, g, lb, norm_g):
    B, T, _ = q.shape
    nc = T // HG_CHUNK
    f = lb + (1.0 - lb) * jax.nn.sigmoid(f_logit)
    log_f = jnp.log(f)
    k = 1.0 - f
    qf = jax.nn.silu(q)

    def to_chunks(a, dh):
        return a.reshape(B, nc, HG_CHUNK, HG_HEADS, dh).transpose(1, 0, 3, 2, 4)

    qc, kc, gc = to_chunks(qf, HG_DK), to_chunks(k, HG_DK), to_chunks(log_f, HG_DK)
    vc = to_chunks(inp, HG_DV)
    causal = jnp.tril(jnp.ones((HG_CHUNK, HG_CHUNK), bool))[:, :, None]

    def step(S, xs):
        qq, kk, vv, ll = xs
        b = jnp.cumsum(ll, axis=2)
        diff = b[:, :, :, None, :] - b[:, :, None, :, :]
        decay = jnp.exp(jnp.where(causal, diff, -jnp.inf))
        attn = jnp.einsum('bhtd,bhsd,bhtsd->bhts', qq, kk, decay)
        o = jnp.einsum('bhts,bhsv->bhtv', attn, vv) + jnp.einsum('bhtd,bhdv->bhtv', qq * jnp.exp(b), S)
        b_last = b[:, :, -1:, :]
        S = jnp.exp(b_last[:, :, 0, :])[..., None] * S + jnp.einsum('bhsd,bhsv->bhdv', kk * jnp.exp(b_last - b), vv)
        return S, o

    S0 = jnp.zeros((B, HG_HEADS, HG_DK, HG_DV), jnp.float32)
    _, o = lax.scan(step, S0, (qc, kc, vc, gc))
    o = o.transpose(1, 0, 3, 2, 4).reshape(B, T, HG_HEADS, HG_DV)
    o = o * lax.rsqrt(jnp.mean(jnp.square(o), -1, keepdims=True) + RMS_EPS)
    return o.reshape(B, T, HG_WIDTH) * norm_g * jax.nn.sigmoid(g)

def nsa_mixer(q, k_c, v_c, k_s, v_s, k_w, v_w, gate_logits,
              pos_k, w1_k, w2_k, pos_v, w1_v, w2_v):
    B, T, _ = q.shape
    G, Hg, dh = NSA_KV_GROUPS, NSA_GROUP_SIZE, NSA_HEAD_DIM
    scale = dh ** -0.5
    slopes = alibi_slopes()
    kv = lambda a: a.reshape(B, T, G, dh)
    k_c, v_c, k_s, v_s, k_w, v_w = map(kv, (k_c, v_c, k_s, v_s, k_w, v_w))

    n_cmp = (T - CMP_BLOCK) // CMP_STRIDE + 1
    tok_idx = jnp.arange(n_cmp)[:, None] * CMP_STRIDE + jnp.arange(CMP_BLOCK)[None, :]

    def compress(a, pos, w1, w2):
        blk = a[:, tok_idx] + pos[None, None, :, None, :]
        blk = blk.transpose(0, 1, 3, 2, 4).reshape(B, n_cmp, G, CMP_BLOCK * dh)
        return jax.nn.gelu(blk @ w1) @ w2

    k_cmp = compress(k_c, pos_k, w1_k, w2_k)
    v_cmp = compress(v_c, pos_v, w1_v, w2_v)
    cmp_end = jnp.arange(n_cmp) * CMP_STRIDE + CMP_BLOCK - 1

    n_slc = T // SLC_BLOCK
    top_n = min(SLC_TOPN, n_slc)
    cs = jnp.arange(n_cmp) * CMP_STRIDE
    ss = jnp.arange(n_slc) * SLC_BLOCK
    overlap = jnp.clip(jnp.minimum(cs[:, None] + CMP_BLOCK, ss[None] + SLC_BLOCK)
                       - jnp.maximum(cs[:, None], ss[None]), 0).astype(jnp.float32) / CMP_BLOCK
    k_slc = k_s.reshape(B, n_slc, SLC_BLOCK, G, dh).transpose(0, 3, 1, 2, 4)
    v_slc = v_s.reshape(B, n_slc, SLC_BLOCK, G, dh).transpose(0, 3, 1, 2, 4)
    gather = jax.vmap(jax.vmap(lambda kb, ix: kb[ix]))

    pad = ((0, 0), (WINDOW, 0), (0, 0), (0, 0))
    kw_pad, vw_pad = jnp.pad(k_w, pad), jnp.pad(v_w, pad)

    nqb = T // Q_BLOCK
    qb = q.reshape(B, nqb, Q_BLOCK, G, Hg, dh).transpose(1, 0, 3, 4, 2, 5)
    gb = jax.nn.sigmoid(gate_logits).reshape(B, nqb, Q_BLOCK, G, Hg, 3).transpose(1, 0, 3, 4, 2, 5)
    j_idx = jnp.arange(n_slc)

    def block_fn(args):
        qi, gi, blk = args
        t = blk * Q_BLOCK + jnp.arange(Q_BLOCK)
        dist_c = (t[:, None] - cmp_end[None, :]).astype(jnp.float32)
        valid_c = dist_c >= 0
        s_c = jnp.einsum('bghtd,bngd->bghtn', qi, k_cmp) * scale - slopes[None, :, :, None, None] * dist_c
        p_c = jax.nn.softmax(jnp.where(valid_c, s_c, NEG), axis=-1) * valid_c
        o_c = jnp.einsum('bghtn,bngd->bghtd', p_c, v_cmp)
        imp = jnp.einsum('bghtn,nj->bgtj', p_c, overlap)
        cur = t[:, None] // SLC_BLOCK
        forced = (j_idx[None] == 0) | (j_idx[None] == cur) | (j_idx[None] == cur - 1)
        imp = jnp.where(forced, FORCE, imp)
        imp = jnp.where(j_idx[None] * SLC_BLOCK <= t[:, None], imp, NEG)
        _, sel = lax.top_k(imp, top_n)
        k_sel = gather(k_slc, sel)
        v_sel = gather(v_slc, sel)
        pos_sel = sel[..., None] * SLC_BLOCK + jnp.arange(SLC_BLOCK)
        dist_s = (t[None, None, :, None, None] - pos_sel)[:, :, None].astype(jnp.float32)
        s_s = jnp.einsum('bghtd,bgtnsd->bghtns', qi, k_sel) * scale - slopes[None, :, :, None, None, None] * dist_s
        s_s = jnp.where(dist_s >= 0, s_s, NEG)
        sh = s_s.shape
        p_s = jax.nn.softmax(s_s.reshape(sh[:4] + (-1,)), axis=-1).reshape(sh)
        o_s = jnp.einsum('bghtns,bgtnsd->bghtd', p_s, v_sel)
        start = blk * Q_BLOCK
        k_win = lax.dynamic_slice_in_dim(kw_pad, start, WINDOW + Q_BLOCK, axis=1)
        v_win = lax.dynamic_slice_in_dim(vw_pad, start, WINDOW + Q_BLOCK, axis=1)
        s_pos = start - WINDOW + jnp.arange(WINDOW + Q_BLOCK)
        dist_w = t[:, None] - s_pos[None]
        valid_w = (dist_w >= 0) & (dist_w < WINDOW) & (s_pos[None] >= 0)
        s_w = jnp.einsum('bghtd,bsgd->bghts', qi, k_win) * scale - slopes[None, :, :, None, None] * dist_w.astype(jnp.float32)
        p_w = jax.nn.softmax(jnp.where(valid_w, s_w, NEG), axis=-1)
        o_w = jnp.einsum('bghts,bsgd->bghtd', p_w, v_win)
        return gi[..., 0:1] * o_c + gi[..., 1:2] * o_s + gi[..., 2:3] * o_w

    out = lax.map(block_fn, (qb, gb, jnp.arange(nqb)))
    return out.transpose(1, 0, 4, 2, 3, 5).reshape(B, T, NSA_WIDTH)

def setup_inputs(seed: int = 0) -> dict:
    key = jax.random.key(seed)
    ks = jax.random.split(key, 24)
    n = lambda k, shape, s: jax.random.normal(k, shape, jnp.float32) * s
    D = D_MODEL
    return {
        "x": n(ks[0], (BATCH, SEQ, D), 1.0),
        "c": n(ks[1], (BATCH, D), 1.0),
        "w_ada": n(ks[2], (DEPTH, D, 6 * D), D ** -0.5),
        "b_ada": n(ks[3], (DEPTH, 6 * D), 0.02),
        "w_in": n(ks[4], (DEPTH, D, IN_COLS), D ** -0.5),
        "hg_lb_logits": n(ks[5], (DEPTH + 1, HG_WIDTH), 1.0),
        "hg_norm_g": 1.0 + n(ks[6], (DEPTH, HG_WIDTH), 0.02),
        "cmp_pos_k": n(ks[7], (DEPTH, CMP_BLOCK, NSA_HEAD_DIM), 0.1),
        "cmp_w1_k": n(ks[8], (DEPTH, CMP_BLOCK * NSA_HEAD_DIM, CMP_HIDDEN), (CMP_BLOCK * NSA_HEAD_DIM) ** -0.5),
        "cmp_w2_k": n(ks[9], (DEPTH, CMP_HIDDEN, NSA_HEAD_DIM), CMP_HIDDEN ** -0.5),
        "cmp_pos_v": n(ks[10], (DEPTH, CMP_BLOCK, NSA_HEAD_DIM), 0.1),
        "cmp_w1_v": n(ks[11], (DEPTH, CMP_BLOCK * NSA_HEAD_DIM, CMP_HIDDEN), (CMP_BLOCK * NSA_HEAD_DIM) ** -0.5),
        "cmp_w2_v": n(ks[12], (DEPTH, CMP_HIDDEN, NSA_HEAD_DIM), CMP_HIDDEN ** -0.5),
        "w_out": n(ks[13], (DEPTH, D, D), D ** -0.5 * BETA),
        "ln1_g": 1.0 + n(ks[14], (DEPTH, D), 0.02),
        "ln1_b": n(ks[15], (DEPTH, D), 0.02),
        "ffn_w1": n(ks[16], (DEPTH, D, D_FF), D ** -0.5),
        "ffn_w3": n(ks[17], (DEPTH, D, D_FF), D ** -0.5),
        "ffn_w2": n(ks[18], (DEPTH, D_FF, D), D_FF ** -0.5 * BETA),
        "ln2_g": 1.0 + n(ks[19], (DEPTH, D), 0.02),
        "ln2_b": n(ks[20], (DEPTH, D), 0.02),
    }

def reference(x, c, w_ada, b_ada, w_in, hg_lb_logits, hg_norm_g,
              cmp_pos_k, cmp_w1_k, cmp_w2_k, cmp_pos_v, cmp_w1_v, cmp_w2_v,
              w_out, ln1_g, ln1_b, ffn_w1, ffn_w3, ffn_w2, ln2_g, ln2_b):
    f32 = jnp.float32
    lower_bounds = jnp.cumsum(jax.nn.softmax(hg_lb_logits.astype(f32), axis=0), axis=0)
    offs = np.cumsum(IN_SIZES)[:-1].tolist()
    for l in range(DEPTH):
        ada = jax.nn.silu(c) @ w_ada[l] + b_ada[l]
        sh1, sc1, g1, sh2, sc2, g2 = jnp.split(ada[:, None, :], 6, axis=-1)
        h = x * (1.0 + sc1) + sh1
        proj = (h @ w_in[l]).astype(f32)
        (hq, hf, hi, hg, nq, nkc, nvc, nks, nvs, nkw, nvw, ngate) = jnp.split(proj, offs, axis=-1)
        y_hg = hgrn2_mixer(hq, hf, hi, hg, lower_bounds[l], hg_norm_g[l].astype(f32))
        y_nsa = nsa_mixer(nq, nkc, nvc, nks, nvs, nkw, nvw, ngate,
                          cmp_pos_k[l].astype(f32), cmp_w1_k[l].astype(f32), cmp_w2_k[l].astype(f32),
                          cmp_pos_v[l].astype(f32), cmp_w1_v[l].astype(f32), cmp_w2_v[l].astype(f32))
        mix = jnp.concatenate([y_hg, y_nsa], axis=-1).astype(x.dtype) @ w_out[l]
        x = layer_norm(ALPHA * x + g1 * mix, ln1_g[l], ln1_b[l])
        h = x * (1.0 + sc2) + sh2
        ffn = (jax.nn.silu(h @ ffn_w1[l]) * (h @ ffn_w3[l])) @ ffn_w2[l]
        x = layer_norm(ALPHA * x + g2 * ffn, ln2_g[l], ln2_b[l])
    return x


_drawn_inputs = setup_inputs


def setup_inputs(seed=0):
    import zlib

    import numpy as np

    out = dict(_drawn_inputs(seed))
    spreads = {}
    factors = {'b_ada': 3.473,
     'hg_lb_logits': 8.0,
     'hg_norm_g': 27.507,
     'cmp_pos_k': 104.691,
     'cmp_w1_k': 9.183,
     'cmp_pos_v': 23.679,
     'ln1_g': 2.815,
     'ln1_b': 2.798,
     'ln2_g': 21.395,
     'ln2_b': 23.07,
     'cmp_w2_k': 3.366}
    for name, (base, spread) in spreads.items():
        noise = np.random.default_rng([zlib.crc32(name.encode()), seed]).standard_normal(out[name].shape)
        drawn = base * np.exp(spread * noise) if base else spread * noise
        out[name] = __import__('jax').numpy.asarray(drawn.astype(out[name].dtype))
    for name, factor in factors.items():
        out[name] = (out[name] * factor).astype(out[name].dtype)
    return out
```

```python
import concourse.bass as bass
from concourse import mybir
import numpy as np

F32, F32R, BF16, I8 = mybir.dt.float32, mybir.dt.float32r, mybir.dt.bfloat16, mybir.dt.int8
ALU = mybir.AluOpType
ACT = mybir.ActivationFunctionType
AX = mybir.AxisListType

P = 128
SEQ, DM = 1024, 1024
KT = DM // P
TT = SEQ // P
HEADS, DH, GROUPS, HG = 8, 64, 2, 4
CMP_STRIDE, CMP_BLOCK, NCMP, CMP_HID = 16, 32, 63, 256
D_FF = 2816
NFF = D_FF // P
WINDOW = 512
ALPHA = 2.0 ** 0.25
LN_EPS, RMS_EPS = 1e-5, 1e-6
NEG = -1e30
FLOOR = 1e29
SLOPES = [2.0 ** -(h + 1) for h in range(HEADS)]
IN_COLS = 3352
C_Q, C_F, C_V, C_G, C_NQ, C_KC, C_VC, C_KS, C_VS, C_KW, C_VW = (
    0, 512, 1024, 1536, 2048, 2560, 2688, 2816, 2944, 3072, 3200)
NGATE = 3 * HEADS
UW = P + NGATE


class Map:

    def __init__(self, nc, base, limit):
        self.nc, self.at, self.limit = nc, (base + 63) // 64 * 64, limit

    def __call__(self, name, shape, dtype=F32):
        size = int(np.prod(shape[1:])) * {F32: 4, F32R: 4, BF16: 2, I8: 1}[dtype]
        t = self.nc.alloc_sbuf_tensor_at(name, shape, dtype, offset=self.at)
        self.at = (self.at + size + 63) // 64 * 64
        assert self.at <= self.limit, (name, self.at, self.limit)
        return t

    def rest(self):
        return Map(self.nc, self.at, self.limit)


class Banks:

    def __init__(self, nc, psum, tag):
        self.psum = psum
        self.filled = [nc.alloc_semaphore(f"{tag}_filled{b}") for b in range(8)]
        self.emptied = [nc.alloc_semaphore(f"{tag}_emptied{b}") for b in range(8)]
        self.turns, self.of, self.next = [0] * 8, {}, {}

    def plan(self, pool, *key):
        i = self.next.get(pool, 0)
        self.next[pool] = i + 1
        b = pool[i % len(pool)]
        self.turns[b] += 1
        self.of[key] = (b, self.turns[b])

    def tile(self, *key):
        return self.psum[self.of[key][0]]

    def begin(self, pe, *key):
        b, n = self.of[key]
        if n > 1:
            pe.wait_ge(self.emptied[b], n - 1)
        return self.psum[b]

    def fill(self, ins, *key):
        ins.then_inc(self.filled[self.of[key][0]], 1)

    def wait_filled(self, eng, *key):
        b, n = self.of[key]
        eng.wait_ge(self.filled[b], n)
        return self.psum[b]

    def empty(self, ins, *key):
        ins.then_inc(self.emptied[self.of[key][0]], 1)

    def wait_emptied(self, eng, *key):
        b, n = self.of[key]
        eng.wait_ge(self.emptied[b], n)


class Chain:

    def __init__(self, eng, sem):
        self.eng, self.sem, self.n = eng, sem, 0

    def tick(self, ins):
        self.n += 1
        ins.then_inc(self.sem, 1)

    def wait(self):
        self.eng.wait_ge(self.sem, self.n)

    def seq(self, ins):
        self.tick(ins)
        self.wait()


def split3(pe, out, a_hi, a_lo, b_hi, b_lo, first, last):
    pe.matmul(out, a_hi, b_hi, start=first, stop=False, skip_group_check=True)
    pe.matmul(out, a_hi, b_lo, start=False, stop=False, skip_group_check=True)
    return pe.matmul(out, a_lo, b_hi, start=False, stop=last, skip_group_check=True)


def program(nc, x, c, w_ada, b_ada, w_in, hg_lb_logits, hg_norm_g, cmp_pos_k, cmp_w1_k, cmp_w2_k,
            cmp_pos_v, cmp_w1_v, cmp_w2_v, w_out, ln1_g, ln1_b, ffn_w1, ffn_w3, ffn_w2, ln2_g, ln2_b, out):
    sem = nc.alloc_semaphore
    psum = [nc.alloc_psum_tensor(f"bank{b}", [P, 512], F32) for b in range(8)]
    top = Map(nc, nc.sbuf_base, nc.sbuf_usable_end)

    ident = top("ident", [P, P])
    ident_bf = top("ident_bf", [P, P], BF16)
    ones = top("ones", [P, P])
    causal_q = top("causal_q", [P, P], BF16)
    causal_k = top("causal_k", [P, P], BF16)
    edge_q = top("edge_q", [P, P], BF16)
    edge_k = top("edge_k", [P, P], BF16)
    cmp_q = top("cmp_q", [P, TT, 64], BF16)
    cmp_k = top("cmp_k", [64, SEQ], BF16)
    cols = top("cols", [P, 108])
    ada = top("ada", [P, 4, KT])
    lb = top("lb", [P, 4])
    oml = top("oml", [P, 4])
    eps = top("eps", [P, 2])
    silu_c = top("silu_c", [P, KT])
    kc_a = top("kc_a", [P, GROUPS, 64], F32R)
    kc_b = top("kc_b", [71, GROUPS, 64], F32R)
    vc_sb = top("vc_sb", [64, GROUPS, 65])
    hcol = top("hcol", [P, 2, KT])
    mix_h_at = top.at
    mix_h = top("mix_h", [P, HG, SEQ])
    hd = [None, None]
    hd_at = top.at
    hd[0] = [top("hd0_f", [P, SEQ]), top("hd0_q", [P, SEQ]), top("hd0_v", [P, TT, P]), top("hd0_g", [P, TT * UW])]
    body = top

    A = body.rest()
    w_raw = A("w_raw", [P, 2, KT, UW])
    w_hi = A("w_hi", [P, 2, KT, UW], F32R)
    w_lo = A("w_lo", [P, 2, KT, UW], F32R)
    R1 = A.rest()
    hgm = A("hgm", [P, 8, P], I8)
    reset = A("reset", [P, SEQ], BF16)
    hd[1] = [A("hd1_f", [P, SEQ]), A("hd1_q", [P, SEQ]), A("hd1_v", [P, TT, P]), A("hd1_g", [P, SEQ])]
    hb = A("hb", [P, SEQ])
    hk = A("hk", [P, SEQ])
    hD = A("hD", [P, 2, SEQ])
    hW = A("hW", [P, 2, SEQ])
    hQb = A("hQb", [P, SEQ])
    hKT = A("hKT", [P, TT, P])
    hS = A("hS", [P, TT, P])
    hAT = A("hAT", [P, 2, 4, P])
    heb = A("heb", [P, TT])
    ho = A("ho", [P, 2, 512])
    ho2 = A("ho2", [P, 2, 512])
    hT_at = A.at
    hT_hi = A("hT_hi", [P, KT, SEQ], F32R)
    hT_lo = A("hT_lo", [P, KT, SEQ], F32R)
    E = R1.rest()
    hgm_room = E("hgm_room", [P, 3 * SEQ // 4])
    x_sb = E("x_sb", [P, TT, DM])
    wa = E("wa", [P, KT, 512])
    E.limit = hT_at
    Cm = R1.rest()
    Cm("hgm_room2", [P, 3 * SEQ // 4])
    a2 = Cm("a2", [P, 2, GROUPS, SEQ])
    w1c = Cm("w1c", [P, 2, 16, CMP_HID])
    w2c = Cm("w2c", [P, 2, 2, DH])
    zc = Cm("zc", [P, 2, 2, 2 * GROUPS * NCMP])
    zb = Cm("zb", [P, 2, 2])
    kst_c = Cm("kst_c", [71, GROUPS, 64])
    assert Cm.at <= hT_at
    B = R1.rest()
    nq = B("nq", [P, 4, SEQ])
    mix_n_at = B.at
    mix_n = B("mix_n", [P, 4, SEQ])
    hold = Map(nc, nc.sbuf_usable_end - 10 * DM * 4 - 64, nc.sbuf_usable_end)
    x1_at = hold.at
    x1 = hold("x1", [P, TT, DM])
    B.limit = hold.at
    gate1 = hold("gate1", [P, DM])
    gate2 = hold("gate2", [P, DM])
    ka_a = B("ka_a", [P, 2, GROUPS, SEQ], F32R)
    ka_b = B("ka_b", [71, 2, GROUPS, SEQ], F32R)
    kp = B("kp", [65, 2, GROUPS, SEQ], F32R)
    kst = [B("kst_s", [71, SEQ]), B("kst_w", [71, SEQ])]
    va = B("va", [P, 2, TT, GROUPS, DH + 1])
    gates = B("gates", [P, TT, NGATE])
    wa2 = B("wa2", [P, 2, KT // 2, 512])
    brow = B("brow", [1, 2 * DM])
    Bl = body.rest()
    Bl.limit = R1.at
    qst = Bl("qst", [DH, HG, P])
    q_a = Bl("q_a", [P, 4, HG * P], F32R)
    q_b = Bl("q_b", [71, 4, HG * P], F32R)
    pt = Bl("pt", [P, 4, HG * P])
    acc2 = Bl("acc2", [P, 512])
    yb = B("yb", [P, 2, 3, HG * DH])
    mx = B("mx", [P, HG, 3])
    negm = B("negm", [P, 2, HG, 7])
    pm = B("pm", [P, HG, 4])
    rc = B("rc", [P, 3, HG])
    C1 = Map(nc, hd_at, mix_n_at)
    wo_raw = C1("wo_raw", [P, 2, KT, 256])
    wo_hi = C1("wo_hi", [P, 2, KT, 256], F32R)
    wo_lo = C1("wo_lo", [P, 2, KT, 256], F32R)
    wt = C1("wt", [P, 2, 512])
    stat = C1("stat", [P, 2, 12])
    mv = C1("mv", [P, TT, 2])
    rstd = C1("rstd", [P, TT, 2])
    C2 = Map(nc, mix_n_at + 4 * SEQ * 4, x1_at)
    mix_hi = C2("mix_hi", [P, KT, SEQ], F32R)
    mix_lo = C2("mix_lo", [P, KT, SEQ], F32R)
    D = Map(nc, mix_h_at, x1_at)
    ln1g = D("ln1g", [P, DM])
    ln1b = D("ln1b", [P, DM])
    h2_hi = D("h2_hi", [P, KT, 512], F32R)
    h2_lo = D("h2_lo", [P, KT, 512], F32R)
    ff_hi = D("ff_hi", [P, NFF, 512], F32R)
    ff_lo = D("ff_lo", [P, NFF, 512], F32R)
    fw_raw = D("fw_raw", [P, 2, DM])
    fw_hi = D("fw_hi", [P, 2, DM], F32R)
    fw_lo = D("fw_lo", [P, 2, DM], F32R)
    ft = D("ft", [P, 2, 512])
    stat2 = D("stat2", [P, 2, 12])
    mv2 = D("mv2", [P, TT, 2])
    rstd2 = D("rstd2", [P, TT, 2])
    T = body.rest()
    prm = T("prm", [108, P])
    acc = T("acc", [P, 512])
    h32 = T("h32", [P, 2, 512])

    bk = Banks(nc, psum, "a")
    bk.plan((7,), "prm")
    for v in range(4):
        bk.plan((7,), "ada", v)
    for m in range(KT):
        for half in range(2):
            bk.plan((0, 1, 2, 3), "xt", m, half)

    consts = sem("consts")
    s_prm, s_c, s_x = sem("prm_loaded"), sem("c_loaded"), [sem("x_loaded0"), sem("x_loaded1")]
    s_wa = sem("ada_weights_loaded")
    s_acc = sem("ada_products_summed")
    s_cols, s_hT = sem("lower_bound_ready"), sem("h_split")
    s_silu = sem("silu_c_ready")
    ch = {e: sem(f"{e}_chain") for e in ("act", "dve", "pool")}
    s_out = sem("out_stored")

    wada_v = w_ada[0].rearrange("(p k) n -> p k n", k=KT)
    ADA = [(1, 0), (1, 1), (0, 0), (0, 1)]

    with nc.Block() as block:
        @block.sync
        def _(sp):
            sp.dma_start(prm[0:48, :], b_ada[0].rearrange("(m p) -> m p", p=P)).then_inc(s_prm, 16)
            sp.dma_start(prm[48:52, :], hg_norm_g[0].rearrange("(m p) -> m p", p=P)).then_inc(s_prm, 16)
            sp.dma_start(prm[52:60, :], hg_lb_logits.rearrange("a (m p) -> (a m) p", p=P)).then_inc(s_prm, 16)
            sp.dma_start(prm[60:76, :], cmp_pos_k[0].rearrange("(m a) d -> m (a d)", a=2)).then_inc(s_prm, 16)
            sp.dma_start(prm[76:92, :], cmp_pos_v[0].rearrange("(m a) d -> m (a d)", a=2)).then_inc(s_prm, 16)
            sp.dma_start(prm[92:100, :], ln1_g[0].rearrange("(m p) -> m p", p=P)).then_inc(s_prm, 16)
            sp.dma_start(prm[100:108, :], ln1_b[0].rearrange("(m p) -> m p", p=P)).then_inc(s_prm, 16)
            sp.dma_start(silu_c[:, :], c[0].rearrange("(p k) -> p k", k=KT)).then_inc(s_c, 16)
            for v, (vec, half) in enumerate(ADA):
                if v:
                    sp.wait_ge(s_acc, v)
                at = vec * DM + half * 512
                sp.dma_start(wa[:, :, :], wada_v[:, :, at:at + 512]).then_inc(s_wa, 16)
                if v < 2:
                    sp.dma_start(x_sb[:, 4 * v:4 * v + 4, :],
                                 x[0, 512 * v:512 * v + 512, :].rearrange("(t p) d -> p t d", p=P)).then_inc(s_x[v], 16)

        @block.gpsimd
        def _(pool):
            own = Chain(pool, ch["pool"])
            own.seq(pool.memset(ident[:, :], 0.0))
            own.seq(pool.affine_select(out=ident[:, :], in_=ident[:, :], compare_op=ALU.not_equal, fill=1.0,
                                       base=0, pattern=[[-1, P]], channel_multiplier=1))
            pool.memset(ones[:, :], 1.0)
            own.seq(pool.memset(eps[:, 0:1], LN_EPS))
            own.seq(pool.memset(eps[:, 1:2], RMS_EPS))
            pool.tensor_copy(ident_bf[:, :], ident[:, :]).then_inc(consts, 1)
            for m in (causal_q, causal_k, edge_q, edge_k, cmp_q, cmp_k):
                own.tick(pool.memset(m[:], 0.0))
            own.tick(pool.memset(reset[:, :], 1.0))
            own.tick(pool.memset(hgm[:, :, :], 0.0))
            own.wait()

            def mask(m, base, pattern, mult):
                own.tick(pool.affine_select(out=m, in_=m, compare_op=ALU.is_ge, fill=NEG, base=base,
                                            pattern=pattern, channel_multiplier=mult))
            mask(causal_q[:, :], 0, [[-1, P]], 1)
            mask(causal_k[:, :], 0, [[1, P]], -1)
            mask(edge_q[:, :], -1, [[1, P]], -1)
            mask(edge_k[:, :], -1, [[-1, P]], 1)
            mask(cmp_q[:, :, :], 1 - CMP_BLOCK, [[P, TT], [-CMP_STRIDE, 64]], 1)
            mask(cmp_k[:, :], 1 - CMP_BLOCK, [[1, SEQ]], -CMP_STRIDE)
            own.tick(pool.memset(reset[:, :].rearrange("p (c t) -> p c t", t=P)[:, :, 0:1], 0.0))
            for i in range(7):
                L = 64 >> i
                up = hgm[:, i, :].rearrange("p (n u l) -> p n u l", u=2, l=L)[:, :, 1, :]
                nb = P // (2 * L)
                own.seq(pool.memset(up, 1.0))
                own.seq(pool.affine_select(out=up, in_=up, compare_op=ALU.is_ge, fill=0.0, base=0,
                                           pattern=[[-2 * L, nb], [0, L]], channel_multiplier=1))
                own.seq(pool.affine_select(out=up, in_=up, compare_op=ALU.is_ge, fill=0.0, base=L - 1,
                                           pattern=[[2 * L, nb], [0, L]], channel_multiplier=-1))
            own.seq(pool.tensor_copy(hgm[:, 7, :], ident[:, :]))

        @block.vector
        def _(dve):
            own = Chain(dve, ch["dve"])
            ps = bk.wait_filled(dve, "prm")
            bk.empty(dve.tensor_copy(cols[:, :], ps[:, 0:108]), "prm")
            bk.wait_emptied(dve, "prm")
            own.seq(dve.tensor_tensor(oml[:, :], cols[:, 52:56], cols[:, 56:60], ALU.subtract))
            dve.wait_ge(s_cols, 1)
            own.seq(dve.tensor_scalar(oml[:, :], lb[:, :], -1.0, 1.0, ALU.mult, ALU.add))
            dve.wait_ge(s_silu, 1)
            for v, (vec, half) in enumerate(ADA):
                dve.wait_ge(s_wa, 16 * (v + 1))
                if v:
                    bk.wait_filled(dve, "ada", v - 1)
                own.seq(dve.tensor_scalar(acc[:, :], wa[:, 0, :], silu_c[:, 0:1], None, ALU.mult))
                for k in range(1, KT):
                    i = dve.scalar_tensor_tensor(acc[:, :], wa[:, k, :], silu_c[:, k:k + 1], acc[:, :], ALU.mult, ALU.add)
                    if k < KT - 1:
                        own.seq(i)
                i.then_inc(s_acc, 1)
                ps = bk.wait_filled(dve, "ada", v)
                bk.empty(dve.scalar_tensor_tensor(ada[:, vec, 4 * half:4 * half + 4], ps[:, 0:4],
                                                  1.0 if vec == 1 else 0.0, cols[:, 8 * vec + 4 * half:8 * vec + 4 * half + 4],
                                                  ALU.add, ALU.add), "ada", v)
            for n in range(2 * KT):
                m, half = n // 2, n % 2
                bk.wait_emptied(dve, "xt", m, half)
                hi = hT_hi[:, m, 512 * half:512 * half + 512]
                own.seq(dve.tensor_copy(hi, h32[:, n % 2, :]))
                dve.tensor_tensor(hT_lo[:, m, 512 * half:512 * half + 512], h32[:, n % 2, :], hi.bitcast(F32),
                                  ALU.subtract).then_inc(s_hT, 1)

        @block.scalar
        def _(act):
            act.wait_ge(s_c, 16)
            act.activation(silu_c[:, :], silu_c[:, :], ACT.Silu).then_inc(s_silu, 1)
            act.wait_ge(ch["dve"], 1)
            act.activation(lb[:, :], oml[:, :], ACT.Sigmoid).then_inc(s_cols, 1)
            bk.wait_emptied(act, "ada", 3)
            for n in range(2 * KT):
                m, half = n // 2, n % 2
                if n >= 2:
                    act.wait_ge(s_hT, n - 1)
                ps = bk.wait_filled(act, "xt", m, half)
                bk.empty(act.activation(h32[:, n % 2, :], ps[:, :], ACT.Identity, bias=ada[:, 0, m:m + 1],
                                        scale=ada[:, 1, m:m + 1]), "xt", m, half)

        @block.tensor
        def _(pe):
            pe.wait_ge(consts, 1)
            pe.wait_ge(s_prm, 112)
            bk.fill(pe.transpose(bk.begin(pe, "prm")[:, 0:108], prm[:, :], ident[0:108, 0:108]), "prm")
            for v in range(4):
                pe.wait_ge(s_acc, v + 1)
                ps = bk.begin(pe, "ada", v)
                for j in range(4):
                    i = pe.matmul(ps[:, j:j + 1], acc[:, j * P:(j + 1) * P], ones[:, 0:1], start=True, stop=True)
                bk.fill(i, "ada", v)
            for m in range(KT):
                for half in range(2):
                    pe.wait_ge(s_x[half], 16)
                    ps = bk.begin(pe, "xt", m, half)
                    for t in range(4):
                        i = pe.transpose(ps[:, t * P:(t + 1) * P], x_sb[:, 4 * half + t, m * P:(m + 1) * P], ident[:, :])
                    bk.fill(i, "xt", m, half)

    units = [(True, C_KC, P), (True, C_VC, P)]
    for h in range(HG):
        units += [(True, C_F + h * P, P), (True, C_Q + h * P, P), (False, C_V + h * P, P), (True, C_G + h * P, P)]
    units += [(True, C_KS, P), (True, C_KW, P), (False, C_VS, P), (False, C_VW, UW)]
    units += [(True, C_NQ + j * P, P) for j in range(4)]
    NU = len(units)
    U_KV, U_NQ = 2 + 4 * HG, 6 + 4 * HG
    def turns(u):
        fm, _, width = units[u]
        return 2 if fm or width == P else 4

    order = []
    for u in range(6):
        order.append(("unit", u))
        if u == 3:
            order.append(("cz", 0))
        if u == 4:
            order += [("cz", 1), ("gelu", 0)]
        if u == 5:
            order += [("gelu", 1), ("ckv",)]
    for h in range(HG):
        n = 6 + 4 * h
        order += [("prep", h), ("ew", h, 0), ("ew", h, 1), ("unit", n), ("kt", h), ("ew", h, 2), ("us", h),
                  ("ew", h, 3), ("gram", h, 2), ("unit", n + 1), ("ew", h, 4), ("gram", h, 3), ("ew", h, 5),
                  ("gram", h, 4), ("unit", n + 2), ("ew", h, 6), ("gram", h, 5), ("ew", h, 7), ("gram", h, 6),
                  ("unit", n + 3), ("ew", h, 8), ("gram", h, 7), ("gram", h, 8), ("gram", h, 9), ("o", h)]
    order += [("unit", u) for u in range(U_NQ, NU)] + [("evac_last",)]

    LOW, HIGH = (0, 1, 2, 3), (4, 5, 6, 7)
    for step in order:
        kind, a = step[0], step[1:]
        if kind == "unit":
            for i in range(turns(a[0])):
                bk.plan(LOW, "u", a[0], i)
        elif kind == "cz":
            bk.plan(HIGH, "cz", a[0])
        elif kind == "ckv":
            bk.plan(HIGH, "ck")
            bk.plan(HIGH, "cv")
        elif kind in ("kt", "us", "gram"):
            for b in range(2):
                bk.plan(HIGH, kind, *a, b)
        elif kind == "o":
            for b in range(2):
                bk.plan(HIGH, "o", a[0], b)
            for b in range(2):
                bk.plan(HIGH, "ss", a[0], b)

    s_w1 = [sem("cmp_weights_loaded0"), sem("cmp_weights_loaded1")]
    s_wraw = [sem("w_raw_loaded0"), sem("w_raw_loaded1")]
    s_whi, s_wlo = sem("w_hi_ready"), sem("w_lo_ready")
    s_kst, s_tanh_in, s_tanh = sem("kst_rows_ready"), sem("tanh_argument_ready"), sem("tanh_ready")
    s_sigq = sem("q_sigmoid_ready")
    s_decay, s_ln = sem("decay_ready"), sem("log_decay_ready")
    s_diff, s_exp, s_w = sem("exponent_ready"), sem("exp_ready"), sem("factor_ready")
    s_state, s_sq, s_rs, s_y = sem("states_ready"), sem("squares_ready"), sem("rms_ready"), sem("y_hg_ready")
    s_mid, s_kc = sem("gelu_ready"), sem("cmp_keys_ready")

    wd = w_in[0].rearrange("(k p) n -> p k n", p=P)
    ch2 = {e: sem(f"{e}_chain_b") for e in ("act", "dve", "pool")}

    def level_views(t, j):
        L = 64 >> (j - 2)
        v = t.rearrange("p (n u l) -> p n u l", u=2, l=L)
        return v[:, :, 0, :], v[:, :, 1, :]

    with nc.Block() as block:
        @block.sync
        def _(sp):
            for kv, (w1, w2) in enumerate(((cmp_w1_k, cmp_w2_k), (cmp_w1_v, cmp_w2_v))):
                if kv == 0:
                    for u in range(2):
                        _, col, width = units[u]
                        sp.dma_start(w_raw[:, u % 2, :, 0:width], wd[:, :, col:col + width]).then_inc(s_wraw[u % 2], 16)
                sp.dma_start(w1c[:, kv, :, :], w1[0].rearrange("(c p) n -> p c n", p=P)).then_inc(s_w1[kv], 16)
                sp.dma_start(w2c[:, kv, :, :], w2[0].rearrange("(c p) n -> p c n", p=P)).then_inc(s_w1[kv], 16)
            for u in range(2, NU):
                _, col, width = units[u]
                sp.wait_ge(s_wlo, u - 1)
                sp.dma_start(w_raw[:, u % 2, :, 0:width], wd[:, :, col:col + width]).then_inc(s_wraw[u % 2], 16)

        @block.gpsimd
        def _(pool):
            own = Chain(pool, ch2["pool"])
            own.seq(pool.memset(kst_c[64:71, :, :], 0.0))
            for row in (1, 4):
                own.seq(pool.affine_select(out=kst_c[64:71, :, :], in_=kst_c[64:71, :, :], compare_op=ALU.not_equal,
                                           fill=1.0, base=-row, pattern=[[0, GROUPS], [0, 64]], channel_multiplier=1))
            pool.iota(kst_c[64:65, :, :], [[0, GROUPS], [CMP_STRIDE, 64]], base=CMP_BLOCK - 1, channel_multiplier=0,
                      allow_small_or_imprecise_dtypes=True).then_inc(s_kst, 1)
            pool.wait_ge(s_kst, 1)
            for u in range(NU):
                width = units[u][2]
                pool.wait_ge(s_whi, u + 1)
                pool.tensor_tensor(w_lo[:, u % 2, :, 0:width], w_raw[:, u % 2, :, 0:width],
                                   w_hi[:, u % 2, :, 0:width].bitcast(F32), ALU.subtract).then_inc(s_wlo, 1)

        @block.tensor
        def _(pe):
            def unit(u):
                fm, _, width = units[u]
                s = u % 2
                pe.wait_ge(s_wlo, u + 1)
                for i in range(turns(u)):
                    ps = bk.begin(pe, "u", u, i)
                    if fm:
                        t = slice(512 * i, 512 * i + 512)
                        for k in range(KT):
                            last = split3(pe, ps[:, :], w_hi[:, s, k, 0:P], w_lo[:, s, k, 0:P], hT_hi[:, k, t], hT_lo[:, k, t],
                                          k == 0, k == KT - 1)
                    else:
                        per = TT // turns(u)
                        for j in range(per):
                            tok = slice((per * i + j) * P, (per * i + j + 1) * P)
                            o = ps[:, j * width:(j + 1) * width]
                            for k in range(KT):
                                last = split3(pe, o, hT_hi[:, k, tok], hT_lo[:, k, tok], w_hi[:, s, k, 0:width],
                                              w_lo[:, s, k, 0:width], k == 0, k == KT - 1)
                    bk.fill(last, "u", u, i)

            def cz(kv):
                pe.wait_ge(s_w1[kv], 32)
                bk.wait_emptied(pe, "u", kv, 1)
                ps = bk.begin(pe, "cz", kv)
                for jt in range(2):
                    for cc in range(16):
                        pe.matmul(ps[:, jt * 126:jt * 126 + 126], w1c[:, kv, cc, jt * P:(jt + 1) * P],
                                  a2[:, kv, :, 2 * cc:2 * cc + CMP_STRIDE * (NCMP - 1) + 1:CMP_STRIDE],
                                  start=cc == 0, stop=cc == 15)
                    for cc in range(16):
                        last = pe.matmul(ps[:, 252 + jt:253 + jt], w1c[:, kv, cc, jt * P:(jt + 1) * P],
                                         cols[:, 60 + 16 * kv + cc:61 + 16 * kv + cc], start=cc == 0, stop=cc == 15)
                bk.fill(last, "cz", kv)

            def ckv():
                pe.wait_ge(s_mid, 1)
                ps = bk.begin(pe, "ck")
                for jt in range(2):
                    last = pe.matmul(ps[0:64, 0:126], w2c[:, 0, jt, :], zc[:, 0, 0, jt * 126:jt * 126 + 126],
                                     start=jt == 0, stop=jt == 1)
                bk.fill(last, "ck")
                pe.wait_ge(s_mid, 2)
                ps = bk.begin(pe, "cv")
                for g in range(GROUPS):
                    for jt in range(2):
                        at = jt * 126 + g * NCMP
                        last = pe.matmul(ps[0:NCMP, g * DH:(g + 1) * DH], zc[:, 1, 0, at:at + NCMP], w2c[:, 1, jt, :],
                                         start=jt == 0, stop=jt == 1)
                bk.fill(last, "cv")

            def kt(h):
                pe.wait_ge(s_w, 9 * h + 2)
                for b in range(2):
                    ps = bk.begin(pe, "kt", h, b)
                    for j in range(4):
                        cc = 4 * b + j
                        last = pe.transpose(ps[:, j * P:(j + 1) * P], hW[:, 1, cc * P:(cc + 1) * P], ident[:, :])
                    bk.fill(last, "kt", h, b)

            def us(h):
                bk.wait_emptied(pe, "u", 4 + 4 * h, 1)
                for b in range(2):
                    bk.wait_emptied(pe, "kt", h, b)
                    ps = bk.begin(pe, "us", h, b)
                    for j in range(4 - b):
                        cc = 4 * b + j
                        last = pe.matmul(ps[:, j * P:(j + 1) * P], hKT[:, cc, :], hd[h % 2][2][:, cc, :], start=True, stop=True)
                    bk.fill(last, "us", h, b)

            def gram(h, j):
                if j <= 8:
                    pe.wait_ge(s_w, 9 * h + j + 1)
                for b in range(2):
                    ps = bk.begin(pe, "gram", h, j, b)
                    for i in range(4):
                        t = slice((4 * b + i) * P, (4 * b + i + 1) * P)
                        l, r = (hW[:, j % 2, t], hW[:, j % 2, t]) if j <= 8 else (hk[:, t], hd[h % 2][1][:, t])
                        last = pe.matmul(ps[:, i * P:(i + 1) * P], l, r, start=True, stop=True)
                    bk.fill(last, "gram", h, j, b)

            def o(h):
                pe.wait_ge(s_state, h + 1)
                v = hd[h % 2][2]
                for b in range(2):
                    bk.wait_emptied(pe, "gram", h, 9, b)
                    ps = bk.begin(pe, "o", h, b)
                    for i in range(4):
                        cc = 4 * b + i
                        last = pe.matmul(ps[:, i * P:(i + 1) * P], v[:, cc, :], hAT[:, b, i, :], start=True, stop=cc == 0)
                        if cc:
                            last = pe.matmul(ps[:, i * P:(i + 1) * P], hS[:, cc, :], hQb[:, cc * P:(cc + 1) * P],
                                             start=False, stop=True)
                    bk.fill(last, "o", h, b)
                for b in range(2):
                    bk.wait_emptied(pe, "o", h, b)
                    bk.fill(pe.matmul(bk.begin(pe, "ss", h, b)[:, :], ones[:, :], ho2[:, b, :], start=True, stop=True),
                            "ss", h, b)

            do = {"unit": unit, "cz": cz, "ckv": ckv, "kt": kt, "us": us, "gram": gram, "o": o}
            for step in order:
                if step[0] in do:
                    do[step[0]](*step[1:])

        @block.scalar
        def _(act):
            own = Chain(act, ch2["act"])

            def take(u):
                width = units[u][2]
                act.wait_ge(s_wraw[u % 2], 16 * (u // 2 + 1))
                if u >= 2:
                    bk.wait_filled(act, "u", u - 2, turns(u - 2) - 1)
                act.activation(w_hi[:, u % 2, :, 0:width], w_raw[:, u % 2, :, 0:width], ACT.Copy).then_inc(s_whi, 1)

            def evac(u):
                if u < 2:
                    return
                h, r = divmod(u - 2, 4)
                if h < HG:
                    hf, hq, hv, hgate = hd[h % 2]
                    if h >= 2 and r == 0:
                        act.wait_ge(s_y, 2 * (h - 1))
                    if h == 1 and r == 0:
                        act.wait_ge(s_kc, 1)
                elif u == U_KV:
                    act.wait_ge(s_y, 2 * (HG - 1))
                elif u == U_NQ:
                    act.wait_ge(s_y, 2 * HG)
                for i in range(turns(u)):
                    ps = bk.wait_filled(act, "u", u, i)
                    t = slice(512 * i, 512 * i + 512)
                    tiles = ps[:, :].rearrange("p (a n) -> p a n", n=P)
                    if h < HG and r == 1:
                        act.activation(hq[:, t], ps[:, :], ACT.Sigmoid).then_inc(s_sigq, 1)
                        continue
                    if h < HG and r == 0:
                        ins = act.activation(hf[:, t], ps[:, :], ACT.Sigmoid)
                    elif h < HG and r == 2:
                        ins = act.activation(hv[:, 4 * i:4 * i + 4, :], tiles, ACT.Copy)
                    elif h < HG:
                        ins = act.activation(hgate[:, t], ps[:, :], ACT.Sigmoid)
                    elif u in (U_KV, U_KV + 1):
                        ins = act.activation(hd[0][u - U_KV][:, t], ps[:, :], ACT.Copy)
                    elif u == U_KV + 2:
                        ins = act.activation(hd[0][2][:, 4 * i:4 * i + 4, :], tiles, ACT.Copy)
                    elif u == U_KV + 3:
                        ins = act.activation(hd[0][3][:, 2 * i * UW:2 * (i + 1) * UW], ps[:, 0:2 * UW], ACT.Copy)
                    else:
                        ins = act.activation(nq[:, u - U_NQ, t], ps[:, :], ACT.Copy)
                    bk.empty(ins, "u", u, i)

            def unit(u):
                if u + 1 < NU:
                    take(u + 1)
                if u:
                    evac(u - 1)

            def gelu(kv):
                act.wait_ge(s_tanh_in, kv + 1)
                act.activation(zc[:, kv, 1, :], zc[:, kv, 1, :], ACT.Tanh, scale=0.7978845608028654).then_inc(s_tanh, 1)

            def prep(h):
                act.wait_ge(s_decay, h + 1)
                act.activation(hb[:, :], hd[h % 2][0][:, :], ACT.Ln).then_inc(s_ln, 1)

            def ew(h, j):
                n = 9 * h + j
                act.wait_ge(s_diff, n + 1)
                d = hD[:, n % 2, :]
                if j == 0:
                    b = hd[h % 2][0]
                    act.activation(heb[:, :], b[:, P - 1::P], ACT.Exp)
                    act.activation(d, b[:, :], ACT.Exp).then_inc(s_exp, 1)
                elif j == 1:
                    act.activation(d, d, ACT.Exp).then_inc(s_exp, 1)
                else:
                    low, up = level_views(d, j)
                    act.activation(low, low, ACT.Exp, scale=-1.0)
                    act.activation(up, up, ACT.Exp).then_inc(s_exp, 1)

            def kt(h):
                if h:
                    bk.wait_filled(act, "us", h - 1, 1)
                for b in range(2):
                    ps = bk.wait_filled(act, "kt", h, b)
                    bk.empty(act.activation(hKT[:, 4 * b:4 * b + 4, :], ps[:, :].rearrange("p (a n) -> p a n", n=P),
                                            ACT.Copy), "kt", h, b)

            def o(h):
                for b in range(2):
                    ps = bk.wait_filled(act, "o", h, b)
                    if h:
                        act.wait_ge(s_y, 2 * (h - 1) + b + 1)
                    act.activation(ho2[:, b, :], ps[:, :], ACT.Square)
                    bk.empty(act.activation(ho[:, b, :], ps[:, :], ACT.Copy), "o", h, b)
                for b in range(2):
                    ps = bk.wait_filled(act, "ss", h, b)
                    bk.empty(act.activation(ho2[:, b, :], ps[:, :], ACT.Ln, scale=1.0 / P, bias=eps[:, 1:2]), "ss", h, b)
                    bk.wait_emptied(act, "ss", h, b)
                    act.activation(ho2[:, b, :], ho2[:, b, :], ACT.Exp, scale=-0.5).then_inc(s_rs, 1)

            take(0)
            do = {"unit": unit, "gelu": gelu, "prep": prep, "ew": ew, "kt": kt, "o": o,
                  "evac_last": lambda: evac(NU - 1)}
            for step in order:
                if step[0] in do:
                    do[step[0]](*step[1:])

        @block.vector
        def _(dve):
            own = Chain(dve, ch2["dve"])
            def evac(u):
                if u < 2:
                    for i in range(2):
                        ps = bk.wait_filled(dve, "u", u, i)
                        skip = 1 - i
                        for g in range(GROUPS):
                            rows = slice(g * DH, (g + 1) * DH)
                            dve.tensor_copy(a2[0:DH, u, g, 512 * i:512 * i + 512], ps[rows, :])
                            ins = dve.tensor_copy(a2[DH:P, u, g, 512 * i - 1 + skip:512 * i + 511], ps[rows, skip:512])
                        bk.empty(ins, "u", u, i)
                elif u < U_KV and (u - 2) % 4 == 1:
                    hq = hd[(u - 2) // 4 % 2][1]
                    for i in range(2):
                        bk.wait_filled(dve, "u", u, i)
                        dve.wait_ge(s_sigq, 2 * ((u - 2) // 4) + i + 1)
                        t = slice(512 * i, 512 * i + 512)
                        bk.empty(dve.tensor_tensor(hq[:, t], hq[:, t], bk.tile("u", u, i)[:, :], ALU.mult), "u", u, i)

            def unit(u):
                if u:
                    evac(u - 1)

            def gelu(kv):
                ps = bk.wait_filled(dve, "cz", kv)
                z, w = zc[:, kv, 0, :], zc[:, kv, 1, :]
                own.seq(dve.tensor_copy(zb[:, kv, :], ps[:, 252:254]))
                for jt in range(2):
                    t = slice(126 * jt, 126 * jt + 126)
                    ins = dve.tensor_scalar(z[:, t], ps[:, t], zb[:, kv, jt:jt + 1], None, ALU.add)
                bk.empty(ins, "cz", kv)
                bk.wait_emptied(dve, "cz", kv)
                own.seq(dve.tensor_tensor(w, z, z, ALU.mult))
                own.seq(dve.tensor_scalar(w, w, 0.044715, 1.0, ALU.mult, ALU.add))
                dve.tensor_tensor(w, w, z, ALU.mult).then_inc(s_tanh_in, 1)
                dve.wait_ge(s_tanh, kv + 1)
                own.seq(dve.scalar_tensor_tensor(z, w, 1.0, z, ALU.add, ALU.mult))
                dve.tensor_scalar(z, z, 0.5, None, ALU.mult).then_inc(s_mid, 1)

            def ckv():
                dve.wait_ge(s_kst, 1)
                own.seq(dve.memset(kst_c[0:64, :, :], 0.0))
                own.seq(dve.memset(vc_sb[:, :, :], 0.0))
                own.tick(dve.memset(vc_sb[:, :, DH:DH + 1], 1.0))
                ps = bk.wait_filled(dve, "ck")
                bk.empty(dve.tensor_copy(kst_c[0:64, :, 0:NCMP], ps[0:64, 0:126].rearrange("p (g n) -> p g n", g=GROUPS)), "ck")
                ps = bk.wait_filled(dve, "cv")
                bk.empty(dve.tensor_copy(vc_sb[0:NCMP, :, 0:DH], ps[0:NCMP, 0:P].rearrange("p (g n) -> p g n", g=GROUPS)), "cv")
                bk.wait_emptied(dve, "cv")
                own.seq(dve.tensor_copy(kc_a[0:64, :, :], kst_c[0:64, :, :]))
                own.tick(dve.tensor_copy(kc_a[64:128, :, :], kc_a[0:64, :, :].bitcast(F32)))
                own.tick(dve.tensor_tensor(kc_b[0:64, :, :], kst_c[0:64, :, :], kc_a[0:64, :, :].bitcast(F32), ALU.subtract))
                own.seq(dve.tensor_copy(kc_b[64:71, :, :], kst_c[64:71, :, :]))
                dve.sem_inc(s_kc, 1)
                own.seq(dve.memset(hAT[:, :, :, :], 0.0))

            def prep(h):
                hf = hd[h % 2][0]
                u = 2 + 4 * h
                for i in range(2):
                    bk.wait_emptied(dve, "u", u, i)
                dve.tensor_scalar(hf[:, :], hf[:, :], oml[:, h:h + 1], lb[:, h:h + 1], ALU.mult, ALU.add).then_inc(s_decay, 1)
                dve.wait_ge(s_decay, h + 1)
                if h:
                    dve.wait_ge(s_w, 9 * h)
                own.tick(dve.tensor_scalar(hk[:, :], hf[:, :], -1.0, 1.0, ALU.mult, ALU.add))
                dve.wait_ge(s_ln, h + 1)
                own.wait()
                dve.tensor_tensor_scan(hf[:, :], reset[:, :], hb[:, :], 0.0, ALU.mult, ALU.add).then_inc(s_diff, 1)
                dve.wait_ge(s_diff, 9 * h + 1)

            def ew(h, j):
                n = 9 * h + j
                b, q = hd[h % 2][0], hd[h % 2][1]
                if n:
                    dve.wait_ge(s_w, n)
                if j < 8:
                    d = hD[:, (n + 1) % 2, :]
                    if j == 0:
                        bc = b[:, :].rearrange("p (c t) -> p c t", t=P)
                        dve.tensor_tensor(d.rearrange("p (c t) -> p c t", t=P), bc[:, :, P - 1:P].to_broadcast([P, TT, P]),
                                          bc, ALU.subtract).then_inc(s_diff, 1)
                    else:
                        L = 64 >> (j - 1)
                        bc = b[:, :].rearrange("p (c t) -> p c t", t=2 * L)
                        dve.tensor_tensor(d.rearrange("p (c t) -> p c t", t=2 * L), bc,
                                          bc[:, :, L - 1:L].to_broadcast([P, SEQ // (2 * L), 2 * L]),
                                          ALU.subtract).then_inc(s_diff, 1)
                dve.wait_ge(s_exp, n + 1)
                d = hD[:, n % 2, :]
                if j == 0:
                    bk.wait_emptied(dve, "u", 3 + 4 * h, 1)
                    if h:
                        bk.wait_filled(dve, "o", h - 1, 1)
                    dve.tensor_tensor(hQb[:, :], q[:, :], d, ALU.mult).then_inc(s_w, 1)
                elif j == 1:
                    if h:
                        bk.wait_filled(dve, "gram", h - 1, 7, 1)
                    dve.tensor_tensor(hW[:, 1, :], hk[:, :], d, ALU.mult).then_inc(s_w, 1)
                else:
                    if j == 2 and h:
                        bk.wait_filled(dve, "gram", h - 1, 8, 1)
                    elif j == 3:
                        bk.wait_filled(dve, "kt", h, 1)
                    elif j > 3:
                        bk.wait_filled(dve, "gram", h, j - 2, 1)
                    wl, wu = level_views(hW[:, j % 2, :], j)
                    dl, du = level_views(d, j)
                    kl, _ = level_views(hk[:, :], j)
                    _, qu = level_views(q[:, :], j)
                    dve.tensor_tensor(wl, kl, dl, ALU.mult)
                    dve.tensor_tensor(wu, qu, du, ALU.mult).then_inc(s_w, 1)

            def us(h):
                if h:
                    bk.wait_filled(dve, "o", h - 1, 1)
                for b in range(2):
                    ps = bk.wait_filled(dve, "us", h, b)
                    for j in range(4 - b):
                        cc = 4 * b + j
                        u = ps[:, j * P:(j + 1) * P]
                        ins = (dve.scalar_tensor_tensor(hS[:, cc + 1, :], hS[:, cc, :], heb[:, cc:cc + 1], u, ALU.mult, ALU.add)
                               if cc else dve.tensor_copy(hS[:, 1, :], u))
                        if j == 3 - b:
                            bk.empty(ins, "us", h, b)
                            bk.wait_emptied(dve, "us", h, b)
                        else:
                            own.seq(ins)
                dve.sem_inc(s_state, 1)

            def gram(h, j):
                if h and j == 2:
                    bk.wait_filled(dve, "o", h - 1, 1)
                for b in range(2):
                    ps = bk.wait_filled(dve, "gram", h, j, b)
                    if j > 2:
                        bk.wait_emptied(dve, "gram", h, j - 1, b)
                    m = hgm[:, j - 2:j - 1, :].to_broadcast([P, 4, P])
                    bk.empty(dve.copy_predicated(hAT[:, b, :, :], m, ps[:, :].rearrange("p (a n) -> p a n", n=P)),
                             "gram", h, j, b)

            def o(h):
                gate = hd[h % 2][3]
                for i in range(2):
                    bk.wait_emptied(dve, "u", 5 + 4 * h, i)
                own.tick(dve.tensor_scalar(gate[:, 0:SEQ], gate[:, 0:SEQ], cols[:, 48 + h:49 + h], None, ALU.mult))
                for b in range(2):
                    dve.wait_ge(s_rs, 2 * h + b + 1)
                    own.seq(dve.tensor_tensor(ho[:, b, :], ho[:, b, :], ho2[:, b, :], ALU.mult))
                    t = slice(512 * b, 512 * b + 512)
                    dve.tensor_tensor(mix_h[:, h, t], ho[:, b, :], gate[:, t], ALU.mult).then_inc(s_y, 1)

            do = {"unit": unit, "gelu": gelu, "ckv": ckv, "prep": prep, "ew": ew, "us": us, "gram": gram, "o": o}
            for step in order:
                if step[0] in do:
                    do[step[0]](*step[1:])

    NIT = 2 * TT
    blocks = []
    for it in range(NIT):
        qt = it // 2
        blocks.append([(0, 0)] + [(1, j) for j in range(qt + 1)] + [(2, j) for j in range(max(0, qt - 4), qt + 1)])
    first = [sum(len(b) for b in blocks[:it]) for it in range(NIT)]

    def chunks(it, br):
        qt = it // 2
        lo, hi = (0 if br == 1 else max(0, qt - 4)) * P, (qt + 1) * P
        return [(a, min(a + 512, hi)) for a in range(lo, hi, 512)]

    at_bk = Banks(nc, psum, "at")
    BR_BANK = (4, 5, 6)
    o_emptied = [sem(f"outputs_read{br}") for br in range(3)]
    ADA2 = [(v, half) for v in (2, 4, 3, 5) for half in range(2)]

    def tickets(it):
        t = []
        for br in (1, 2):
            for i, (a, b) in enumerate(chunks(it, br)):
                n = {128: 4, 256: 2}.get(b - a, 1)
                t += [(h0, n, br, i, a, b) for h0 in range(0, HG, n)]
        return t + [None]

    flat = [(it, b) for it in range(NIT) for b in range(len(blocks[it]))]
    steps = [("keys", 0), ("keys", 1), ("qprep", 0), ("keys", 2), ("keys", 3), ("qprep", 1), ("values",), ("qprep", 2)]
    for it in range(2):
        steps += [("p1", it, k) for k in range(len(tickets(it)))] + [("maxend", it)]
    steps += [("m4", 0), ("qaug", 0), ("m4", 1), ("qaug", 1), ("S", 0, 0), ("S", 0, 1)]
    late = []
    for v in range(len(ADA2)):
        late += [[("acc2", v, k)] for k in range(KT)]
        if v:
            late[-KT] = [("ada2", v - 1), ("ada2_out", v - 1)] + late[-KT]
    late.append([("ada2", len(ADA2) - 1), ("ada2_out", len(ADA2) - 1)])
    for n0 in range(0, len(flat), 2):
        pair = [(n,) + flat[n] for n in (n0, n0 + 1)]
        if pair[0][2] == 0 and 2 <= pair[0][1] + 1 < NIT:
            steps += [("m4", pair[0][1] + 1), ("qaug", pair[0][1] + 1)]
        steps += [("S",) + flat[n + 2] for n, it, b in pair if n + 2 < len(flat)]
        for n, it, b in pair:
            if it + 2 < NIT:
                k, nb = len(tickets(it + 2)), max(2, len(blocks[it]) - 2)
                if b:
                    steps += [("p1", it + 2, i) for i in range(min(k, k * (b - 1) // nb), min(k, k * b // nb))]
                if b == nb:
                    steps.append(("maxend", it + 2))
                if b == len(blocks[it]) - 1 and it + 3 < NIT:
                    steps.append(("qprep", it + 3))
        for n, it, b in pair:
            if n == n0 + 1 and b == 0 and 2 <= it + 1 < NIT:
                steps += [("m4", it + 1), ("qaug", it + 1)]
            steps.append(("pv", it, b))
            if b == len(blocks[it]) - 1 or blocks[it][b + 1][0] != blocks[it][b][0]:
                steps.append(("combine", it, blocks[it][b][0]))
            if b == 1 and it:
                steps += [("yt", it - 1)]
            if n >= 8 and n % 2 == 0 and (n - 8) // 2 < len(late):
                steps += late[(n - 8) // 2]
    steps.append(("yt", NIT - 1))
    assert (len(flat) - 8) // 2 >= len(late)
    for step in steps:
        if step[0] == "p1":
            at_bk.plan((0, 1), *step)
        elif step[0] == "S":
            at_bk.plan((2, 3), *step)
        elif step[0] in ("m4", "yt", "ada2"):
            at_bk.plan((7,), *step)

    s_rows, s_kb, s_kp = [sem("bias_rows_ready0"), sem("bias_rows_ready1")], sem("keys_low_ready"), sem("keys_high_ready")
    s_ka, s_slope = sem("keys_doubled"), sem("slopes_ready")
    s_va, s_gates = sem("values_ready"), sem("gates_ready")
    s_q, s_negm, s_qaug = sem("queries_split"), sem("maxima_ready"), sem("maxima_in_queries")
    s_pv, s_ytok = sem("probs_used"), sem("y_nsa_ready")
    s_wa2 = [sem("ada2_loaded0"), sem("ada2_loaded1")]
    s_acc2, s_half, s_brow = sem("ada2_summed"), sem("ada2_half_used"), sem("brow_loaded")
    ch3 = {e: sem(f"{e}_chain_c") for e in ("act", "dve", "pool")}
    vw = hd[0][3][:, :].rearrange("p (a n) -> p a n", n=UW)

    with nc.Block() as block:
        @block.sync
        def _(sp):
            sp.dma_start(brow[:, 0:DM], b_ada[:, 2 * DM:3 * DM]).then_inc(s_brow, 16)
            sp.dma_start(brow[:, DM:2 * DM], b_ada[:, 5 * DM:6 * DM]).then_inc(s_brow, 16)
            for w in range(2 * len(ADA2)):
                vec, half = ADA2[w // 2]
                if w >= 2:
                    sp.wait_ge(s_half, w - 1)
                at, k = vec * DM + half * 512, (w % 2) * (KT // 2)
                sp.dma_start(wa2[:, w % 2, :, :], wada_v[:, k:k + KT // 2, at:at + 512]).then_inc(s_wa2[w % 2], 16)

        @block.gpsimd
        def _(pool):
            own = Chain(pool, ch3["pool"])
            for br in range(2):
                rows = kst[br][64:71, :]
                own.seq(pool.memset(rows, 0.0))
                for row in (2 + br, 5 + br):
                    own.seq(pool.affine_select(out=rows, in_=rows, compare_op=ALU.not_equal, fill=1.0, base=-row,
                                               pattern=[[0, SEQ]], channel_multiplier=1))
                pool.iota(kst[br][64:65, :], [[1, SEQ]], base=0, channel_multiplier=0,
                          allow_small_or_imprecise_dtypes=True).then_inc(s_rows[br], 1)
                if br == 0:
                    for g in range(GROUPS):
                        for hh in range(HG):
                            pool.memset(mix_n[64:65, g, hh * P:(hh + 1) * P], SLOPES[4 * g + hh]).then_inc(s_slope, 1)
                    pool.wait_ge(s_rows[0], 1)
            pool.wait_ge(s_rows[1], 1)
            pool.wait_ge(s_slope, 2 * HG)
            for g in range(GROUPS):
                for hh in range(HG):
                    own.tick(pool.memset(negm[:, g, hh, 0:1], SLOPES[4 * g + hh]))
            own.tick(pool.memset(va[:, :, :, :, DH:DH + 1], 1.0))

        @block.tensor
        def _(pe):
            def p1(it, n):
                qt, g = divmod(it, 2)
                s = it % 4
                if n == 0:
                    pe.wait_ge(s_q, it + 1)
                    pe.wait_ge(s_kp, 2 * g + 2)
                ps = at_bk.begin(pe, "p1", it, n)
                if tickets(it)[n] is None:
                    for hh in range(HG):
                        o = ps[:, hh * 64:(hh + 1) * 64]
                        pe.matmul(o, q_a[:, s, hh * P:(hh + 1) * P], kc_a[:, g, :], start=True, stop=False,
                                  skip_group_check=True)
                        pe.matmul(o, q_b[0:65, s, hh * P:(hh + 1) * P], kc_b[0:65, g, :], start=False, stop=False,
                                  skip_group_check=True)
                        last = pe.matmul(o, ident_bf[:, :], cmp_q[:, qt, :], start=False, stop=True, skip_group_check=True)
                else:
                    h0, heads, br, i, a, b = tickets(it)[n]
                    masks = [(qt, causal_q)] + ([(qt - 4, edge_q)] if br == 2 and qt >= 4 else [])
                    masks = [(j, m) for j, m in masks if a <= j * P < b]
                    for hh in range(heads):
                        at = hh * (b - a)
                        last = pe.matmul(ps[:, at:at + b - a], q_b[0:65, s, (h0 + hh) * P:(h0 + hh + 1) * P],
                                         kp[:, br - 1, g, a:b], start=True, stop=not masks, skip_group_check=True)
                        for j, m in masks:
                            last = pe.matmul(ps[:, at + j * P - a:at + j * P - a + P], ident_bf[:, :], m[:, :], start=False,
                                             stop=j == masks[-1][0], skip_group_check=True)
                at_bk.fill(last, "p1", it, n)

            def m4(it):
                pe.wait_ge(s_negm, it + 1)
                ps = at_bk.begin(pe, "m4", it)
                for hh in range(HG):
                    last = pe.matmul(ps[64:71, hh * P:(hh + 1) * P], negm[:, it % 2, hh, :], ident[:, :], start=True, stop=True)
                at_bk.fill(last, "m4", it)

            def S(it, b):
                qt, g = divmod(it, 2)
                br, j = blocks[it][b]
                s = it % 4
                if b == 0:
                    pe.wait_ge(s_qaug, it + 1)
                elif b == 1:
                    pe.wait_ge(s_kb, 2 * g + 2)
                    pe.wait_ge(s_ka, 2 * g + 2)
                ps = at_bk.begin(pe, "S", it, b)
                if br == 0:
                    o, k_a, k_b = ps[0:64, :], kc_a[:, g, :], kc_b[:, g, :]
                    masks = [cmp_k[:, qt * P:(qt + 1) * P]]
                else:
                    keys = slice(j * P, (j + 1) * P)
                    o, k_a, k_b = ps[:, :], ka_a[:, br - 1, g, keys], ka_b[:, br - 1, g, keys]
                    masks = [causal_k[:, :]] * (j == qt) + [edge_k[:, :]] * (br == 2 and j == qt - 4)
                n = o.shape[0]
                pe.matmul(o, k_a, q_a[:, s, :], start=True, stop=False, skip_group_check=True)
                last = pe.matmul(o, k_b, q_b[:, s, :], start=False, stop=not masks, skip_group_check=True)
                for i, m in enumerate(masks):
                    last = pe.matmul(o.rearrange("k (h q) -> k h q", h=HG), ident_bf[0:n, 0:n],
                                     m.unsqueeze(1).to_broadcast([n, HG, P]), start=False, stop=i == len(masks) - 1,
                                     skip_group_check=True)
                at_bk.fill(last, "S", it, b)

            def pv(it, b):
                qt, g = divmod(it, 2)
                br, j = blocks[it][b]
                n = first[it] + b
                if n == 0:
                    pe.wait_ge(s_va, 5)
                at_bk.wait_emptied(pe, "S", it, b)
                starts = b == 0 or blocks[it][b - 1][0] != br
                if starts and it:
                    pe.wait_ge(o_emptied[br], it)
                stops = b == len(blocks[it]) - 1 or blocks[it][b + 1][0] != br
                rows = 64 if br == 0 else P
                v = vc_sb[:, g, :] if br == 0 else va[:, br - 1, j, g, :]
                for hh in range(HG):
                    last = pe.matmul(psum[BR_BANK[br]][:, hh * 65:(hh + 1) * 65], pt[0:rows, n % 4, hh * P:(hh + 1) * P], v,
                                     start=starts and hh == 0, stop=stops, skip_group_check=True)
                last.then_inc(s_pv, 1)

            def yt(it):
                pe.wait_ge(s_ytok, it + 1)
                ps = at_bk.begin(pe, "yt", it)
                for j in range(2):
                    last = pe.transpose(ps[:, j * P:(j + 1) * P], yb[:, it % 2, 0, j * P:(j + 1) * P], ident[:, :])
                at_bk.fill(last, "yt", it)

            def ada2(v):
                vec, half = ADA2[v]
                pe.wait_ge(s_acc2, v + 1)
                ps = at_bk.begin(pe, "ada2", v)
                if vec in (3, 4):
                    for j in range(4):
                        last = pe.matmul(ps[:, j:j + 1], acc2[:, j * P:(j + 1) * P], ones[:, 0:1], start=True, stop=True)
                else:
                    at = (vec == 5) * DM + half * 512
                    pe.wait_ge(s_brow, 32)
                    pe.matmul(ps[:, :], ones[:, :], acc2[:, :], start=True, stop=False)
                    last = pe.matmul(ps[:, :], ones[0:1, :], brow[:, at:at + 512], start=False, stop=True)
                at_bk.fill(last, "ada2", v)

            do = {"p1": p1, "m4": m4, "S": S, "pv": pv, "yt": yt, "ada2": ada2}
            for step in steps:
                if step[0] in do:
                    do[step[0]](*step[1:])

        @block.scalar
        def _(act):
            def mix(it):
                qt, g = divmod(it, 2)
                ps = at_bk.wait_filled(act, "yt", it)
                at_bk.empty(act.activation(mix_n[:, 2 * g:2 * g + 2, qt * P:(qt + 1) * P],
                                           ps[:, 0:2 * P].rearrange("p (j t) -> p j t", j=2), ACT.Copy), "yt", it)

            act.activation(gates[:, :, :], vw[:, :, P:UW], ACT.Sigmoid).then_inc(s_gates, 1)
            def weights(it, b):
                n = first[it] + b
                ps = at_bk.wait_filled(act, "S", it, b)
                if n >= 4:
                    act.wait_ge(s_pv, n - 3)
                rows = 64 if blocks[it][b][0] == 0 else P
                at_bk.empty(act.activation(pt[0:rows, n % 4, :], ps[0:rows, :], ACT.Exp), "S", it, b)

            def keys(n):
                g, br = divmod(n, 2)
                act.wait_ge(s_kp, n + 1)
                act.activation(ka_b[64:71, br, g, :], kst[br][64:71, :], ACT.Copy).then_inc(ch3["act"], 1)
                act.activation(ka_a[0:64, br, g, :], kp[0:64, br, g, :].bitcast(F32), ACT.Copy).then_inc(ch3["act"], 1)
                act.activation(ka_a[64:128, br, g, :], kp[0:64, br, g, :].bitcast(F32), ACT.Copy).then_inc(s_ka, 1)

            do = {"keys": keys, "S": weights, "yt": mix}
            for step in steps:
                if step[0] in do:
                    do[step[0]](*step[1:])

        @block.vector
        def _(dve):
            own = Chain(dve, ch3["dve"])

            def keys(n):
                g, br = divmod(n, 2)
                dve.wait_ge(s_rows[br], 1)
                own.seq(dve.tensor_copy(kst[br][0:DH, :], hd[0][br][g * DH:(g + 1) * DH, :]))
                dve.tensor_copy(kp[:, br, g, :], kst[br][0:65, :]).then_inc(s_kp, 1)
                dve.wait_ge(s_kp, n + 1)
                dve.tensor_tensor(ka_b[0:64, br, g, :], kst[br][0:64, :], kp[0:64, br, g, :].bitcast(F32),
                                  ALU.subtract).then_inc(s_kb, 1)
                dve.wait_ge(s_kb, n + 1)

            def qprep(it):
                qt, g = divmod(it, 2)
                s = it % 4
                tok = slice(qt * P, (qt + 1) * P)
                own.wait()
                for par in range(2):
                    own.tick(dve.tensor_scalar(qst[:, par::2, :], nq[par * DH:(par + 1) * DH, 2 * g:2 * g + 2, tok],
                                               DH ** -0.5, None, ALU.mult))
                own.wait()
                if it >= 4:
                    at_bk.wait_filled(dve, "S", it - 4, len(blocks[it - 4]) - 1)
                q = qst[:, :, :].rearrange("p h t -> p (h t)")
                if it < 4:
                    dve.wait_ge(s_slope, 2 * HG)
                    own.tick(dve.tensor_copy(q_b[64:65, s, :], mix_n[64:65, g, 0:HG * P]))
                own.seq(dve.tensor_copy(q_a[0:64, s, :], q))
                own.tick(dve.tensor_copy(q_b[0:64, s, :], q_a[0:64, s, :].bitcast(F32)))
                own.tick(dve.tensor_tensor(q_a[64:128, s, :], q, q_a[0:64, s, :].bitcast(F32), ALU.subtract))
                own.wait()
                dve.sem_inc(s_q, 1)

            def values():
                for br in range(2):
                    src = (hd[0][2][:, :, :] if br == 0 else vw[:, :, 0:P]).rearrange("p t (g d) -> p t g d", g=GROUPS)
                    for g in range(GROUPS):
                        dve.tensor_copy(va[:, br, :, g, 0:DH], src[:, :, g, :]).then_inc(s_va, 1)
                dve.wait_ge(ch3["pool"], 6 + 8 + 1)
                dve.sem_inc(s_va, 1)

            def maxima(it, n):
                ps = at_bk.wait_filled(dve, "p1", it, n)
                if tickets(it)[n] is None:
                    x, o, neg = ps[:, 0:HG * 64].rearrange("p (h n) -> p h n", h=HG), mx[:, :, 0:1], True
                else:
                    h0, heads, br, i, a, b = tickets(it)[n]
                    x = ps[:, 0:heads * (b - a)].rearrange("p (h n) -> p h n", h=heads)
                    o, neg = pm[:, h0:h0 + heads, 2 * (br - 1) + i:2 * (br - 1) + i + 1], False
                at_bk.empty(dve.tensor_reduce(o, x, axis=AX.X, op=ALU.max, negate=neg), "p1", it, n)

            def maxend(it):
                g = it % 2
                for n in (-1, -2):
                    at_bk.wait_emptied(dve, "p1", it, len(tickets(it)) + n)
                own.tick(dve.tensor_scalar(mx[:, :, 0:1], mx[:, :, 0:1], FLOOR, None, ALU.min))
                for br in (1, 2):
                    n = len(chunks(it, br))
                    own.tick(dve.tensor_reduce(mx[:, :, br:br + 1], pm[:, :, 2 * (br - 1):2 * (br - 1) + n], axis=AX.X,
                                               op=ALU.max, negate=True))
                own.wait()
                if it >= 2:
                    at_bk.wait_filled(dve, "m4", it - 2)
                else:
                    dve.wait_ge(ch3["pool"], 6 + 8)
                own.seq(dve.tensor_copy(negm[:, g, :, 1:4].bitcast(F32R), mx[:, :, :]))
                own.tick(dve.tensor_tensor(negm[:, g, :, 4:7], mx[:, :, :], negm[:, g, :, 1:4], ALU.subtract))
                own.wait()
                dve.sem_inc(s_negm, 1)

            def qaug(it):
                ps = at_bk.wait_filled(dve, "m4", it)
                at_bk.empty(dve.tensor_copy(q_b[64:71, it % 4, :], ps[64:71, :]), "m4", it)
                at_bk.wait_emptied(dve, "m4", it)
                dve.sem_inc(s_qaug, 1)

            def combine(it, br):
                qt, g = divmod(it, 2)
                y = yb[:, it % 2, :, :]
                if it >= 2 and br == 0:
                    at_bk.wait_filled(dve, "yt", it - 2)
                if it == 0 and br == 0:
                    dve.wait_ge(s_gates, 1)
                dve.wait_ge(s_pv, first[it] + 1 + max(b for b in range(len(blocks[it])) if blocks[it][b][0] == br))
                o = psum[BR_BANK[br]][:, 0:HG * 65].rearrange("p (h n) -> p h n", h=HG)
                r = rc[:, br, :]
                own.seq(dve.tensor_scalar(r, o[:, :, DH:DH + 1].rearrange("p h n -> p (h n)"), 1e-30, None, ALU.max))
                own.seq(dve.reciprocal(r, r))
                gt = gates[:, qt, :].rearrange("p (h b) -> p b h", b=3)[:, br, HG * g:HG * g + HG]
                own.seq(dve.tensor_tensor(r, r, gt, ALU.mult))
                dve.tensor_tensor(y[:, br, :].rearrange("p (h n) -> p h n", h=HG), o[:, :, 0:DH],
                                  r.unsqueeze(2).to_broadcast([P, HG, DH]), ALU.mult).then_inc(o_emptied[br], 1)
                dve.wait_ge(o_emptied[br], it + 1)
                if br == 1:
                    own.seq(dve.tensor_tensor(y[:, 0, :], y[:, 0, :], y[:, 1, :], ALU.add))
                elif br == 2:
                    dve.tensor_tensor(y[:, 0, :], y[:, 0, :], y[:, 2, :], ALU.add).then_inc(s_ytok, 1)

            def acc2_step(v, k):
                kh, kk = divmod(k, KT // 2)
                if kk == 0:
                    dve.wait_ge(s_wa2[kh], 16 * (v + 1))
                if k == 0:
                    if v:
                        at_bk.wait_filled(dve, "ada2", v - 1)
                    own.tick(dve.tensor_scalar(acc2[:, :], wa2[:, 0, 0, :], silu_c[:, 0:1], None, ALU.mult))
                    return
                own.wait()
                i = dve.scalar_tensor_tensor(acc2[:, :], wa2[:, kh, kk, :], silu_c[:, k:k + 1], acc2[:, :], ALU.mult, ALU.add)
                if kk < KT // 2 - 1:
                    own.tick(i)
                    return
                i.then_inc(s_half, 1)
                dve.wait_ge(s_half, 2 * v + kh + 1)
                if kh:
                    dve.sem_inc(s_acc2, 1)

            def ada2_out(v):
                vec, half = ADA2[v]
                ps = at_bk.wait_filled(dve, "ada2", v)
                if vec in (3, 4):
                    j = slice(4 * half, 4 * half + 4)
                    ins = dve.scalar_tensor_tensor(ada[:, vec - 1, j], ps[:, 0:4], 1.0 if vec == 4 else 0.0,
                                                   cols[:, 8 * vec + 4 * half:8 * vec + 4 * half + 4], ALU.add, ALU.add)
                else:
                    ins = dve.tensor_copy((gate1 if vec == 2 else gate2)[:, 512 * half:512 * half + 512], ps[:, :])
                at_bk.empty(ins, "ada2", v)

            do = {"keys": keys, "values": values, "qprep": qprep, "p1": maxima, "maxend": maxend, "qaug": qaug, "combine": combine,
                  "acc2": acc2_step, "ada2_out": ada2_out}
            for step in steps:
                if step[0] in do:
                    do[step[0]](*step[1:])

    wo_bk = Banks(nc, psum, "wo")
    for u in range(4):
        for pr in range(4):
            wo_bk.plan(tuple(range(8)), u, pr)
    s_x1 = sem("x_reloaded")
    s_wo, s_wohi, s_wolo = [sem("wo_loaded0"), sem("wo_loaded1")], sem("wo_hi_ready"), sem("wo_lo_ready")
    s_mhi, s_mlo = sem("mix_hi_ready"), sem("mix_lo_ready")
    s_mv, s_ln, s_rstd, s_xn = sem("moments_ready"), sem("ln_ready"), sem("rstd_ready"), sem("normalized")
    ch4 = {e: sem(f"{e}_chain_d") for e in ("act", "dve", "pool")}
    wov = w_out[0].rearrange("(k p) n -> p k n", p=P)

    def mix_src(k):
        return mix_h[:, k, :] if k < HG else mix_n[:, k - HG, :]

    with nc.Block() as block:
        @block.sync
        def _(sp):
            for u in range(4):
                if u >= 2:
                    sp.wait_ge(s_wolo, u - 1)
                sp.dma_start(wo_raw[:, u % 2, :, :], wov[:, :, 256 * u:256 * u + 256]).then_inc(s_wo[u % 2], 16)
                if u == 1:
                    sp.dma_start(x1[:, :, :], x[0].rearrange("(t p) d -> p t d", p=P)).then_inc(s_x1, 16)

        @block.gpsimd
        def _(pool):
            for u in range(4):
                pool.wait_ge(s_wohi, u + 1)
                pool.tensor_tensor(wo_lo[:, u % 2, :, :], wo_raw[:, u % 2, :, :], wo_hi[:, u % 2, :, :].bitcast(F32),
                                   ALU.subtract).then_inc(s_wolo, 1)

        @block.tensor
        def _(pe):
            for u in range(4):
                pe.wait_ge(s_wolo, u + 1)
                for pr in range(4):
                    ps = wo_bk.begin(pe, u, pr)
                    for j in range(2):
                        tok = slice((2 * pr + j) * P, (2 * pr + j + 1) * P)
                        for k in range(KT):
                            if u == 0 and pr == 0 and j == 0:
                                pe.wait_ge(s_mlo, k + 1)
                            last = split3(pe, ps[:, 256 * j:256 * j + 256], mix_hi[:, k, tok], mix_lo[:, k, tok],
                                          wo_hi[:, u % 2, k, :], wo_lo[:, u % 2, k, :], k == 0, k == KT - 1)
                    wo_bk.fill(last, u, pr)

        @block.scalar
        def _(act):
            def take(u):
                act.wait_ge(s_wo[u % 2], 16 * (u // 2 + 1))
                if u >= 2:
                    wo_bk.wait_filled(act, u - 2, 3)
                act.activation(wo_hi[:, u % 2, :, :], wo_raw[:, u % 2, :, :], ACT.Copy).then_inc(s_wohi, 1)

            for k in range(KT):
                act.activation(mix_hi[:, k, :], mix_src(k), ACT.Copy).then_inc(s_mhi, 1)
                if k == 1:
                    take(0)
            for u in range(1, 4):
                take(u)
            for pr in range(4):
                act.wait_ge(s_mv, pr + 1)
                t = slice(2 * pr, 2 * pr + 2)
                act.activation(rstd[:, t, 0:1], mv[:, t, 1:2], ACT.Ln, bias=eps[:, 0:1]).then_inc(s_ln, 1)
                act.wait_ge(s_ln, 2 * pr + 1)
                act.activation(rstd[:, t, 0:1], rstd[:, t, 0:1], ACT.Exp, scale=-0.5).then_inc(s_ln, 1)
                act.wait_ge(s_rstd, pr + 1)
                for j in range(2):
                    i = 2 * pr + j
                    act.activation(x1[:, i, :], x1[:, i, :], ACT.Identity, scale=rstd[:, i, 0:1], bias=rstd[:, i, 1:2])\
                       .then_inc(s_xn, 1)

        @block.vector
        def _(dve):
            own = Chain(dve, ch4["dve"])

            def nmr(pr):
                t = slice(2 * pr, 2 * pr + 2)
                dve.wait_ge(s_ln, 2 * pr + 2)
                dve.scalar_tensor_tensor(rstd[:, t, 1:2], mv[:, t, 0:1], -1.0, rstd[:, t, 0:1], ALU.mult, ALU.mult)\
                   .then_inc(s_rstd, 1)

            for k in range(KT):
                dve.wait_ge(s_mhi, k + 1)
                dve.tensor_tensor(mix_lo[:, k, :], mix_src(k), mix_hi[:, k, :].bitcast(F32), ALU.subtract).then_inc(s_mlo, 1)
            own.tick(dve.tensor_tensor(hcol[:, 0, :], cols[:, 92:100], ada[:, 3, :], ALU.mult))
            own.seq(dve.tensor_tensor(hcol[:, 1, :], cols[:, 100:108], ada[:, 3, :], ALU.mult))
            own.tick(dve.tensor_tensor(hcol[:, 1, :], hcol[:, 1, :], ada[:, 2, :], ALU.add))
            dve.wait_ge(s_x1, 16)
            for u in range(4):
                cs = slice(256 * u, 256 * u + 256)
                for pr in range(4):
                    ps = wo_bk.wait_filled(dve, u, pr)
                    n = 4 * u + pr
                    if n >= 2:
                        own.wait()
                    t = wt[:, n % 2, :].rearrange("p (a n) -> p a n", a=2)
                    wo_bk.empty(dve.tensor_tensor(t, ps[:, :].rearrange("p (a n) -> p a n", a=2),
                                                  gate1[:, cs].unsqueeze(1).to_broadcast([P, 2, 256]), ALU.mult), u, pr)
                    wo_bk.wait_emptied(dve, u, pr)
                    xs = x1[:, 2 * pr:2 * pr + 2, cs]
                    own.tick(dve.scalar_tensor_tensor(xs, xs, ALPHA, t, ALU.mult, ALU.add))
                    if u == 3:
                        own.wait()
                        for j in range(2):
                            i = 2 * pr + j
                            for q in range(2):
                                own.tick(dve.bn_stats(stat[:, j, 6 * q:6 * q + 6], x1[:, i, 512 * q:512 * q + 512]))
                            own.wait()
                            ins = dve.bn_aggr(mv[:, i, :], stat[:, j, :])
                            if j == 0:
                                own.tick(ins)
                        ins.then_inc(s_mv, 1)
                        if pr:
                            nmr(pr - 1)
            nmr(3)

    NUP, NUNITS = 2 * NFF, 3 * NFF
    s_fraw = [sem("fw_loaded0"), sem("fw_loaded1")]
    s_fhi = sem("fw_hi_ready")
    s_flo = sem("fw_lo_ready_plus_2")
    s_fused = sem("fw_units_used_plus_2")
    s_silu2, s_prod, s_ffhi = sem("silu_ready"), sem("product_ready"), sem("ff_hi_ready")
    s_ff = sem("ff_tiles_ready_plus_2")
    s_tr, s_tre, s_h2 = sem("h2_transposed"), sem("h2_turned_read"), sem("h2_split")
    s_dn = sem("down_banks_read")
    s_mv2, s_ln2, s_rstd2, s_xn2 = sem("moments2_ready"), sem("ln2_ready"), sem("rstd2_ready"), sem("normalized2")
    s_lnp, s_lnp2, s_res, s_fin = sem("ln_rows_loaded"), sem("ln2_rows_loaded"), sem("residual_ready"), sem("rows_ready")
    ch5 = {e: sem(f"{e}_chain_e") for e in ("act", "dve", "pool")}
    w1v = ffn_w1[0].rearrange("(k p) n -> p k n", p=P)
    w3v = ffn_w3[0].rearrange("(k p) n -> p k n", p=P)

    def kcols(t):
        return t.rearrange("p (k n) -> p k n", n=P)

    with nc.Block() as block:
        @block.sync
        def _(sp):
            def load(slot, src, after):
                sp.wait_ge(s_flo, after)
                sp.dma_start(kcols(fw_raw[:, slot, :]) if len(src.shape) == 3 else fw_raw[:, slot, :], src)\
                  .then_inc(s_fraw[slot], 16)
            sp.dma_start(ln1g[:, :], ln1_g.to_broadcast([P, DM])).then_inc(s_lnp, 16)
            sp.dma_start(ln1b[:, :], ln1_b.to_broadcast([P, DM])).then_inc(s_lnp, 16)
            for half in range(2):
                u0 = half * NUNITS
                with sp.Fori(0, NFF) as f:
                    load(0, w1v[:, :, bass.ds(f * P, P)], u0 + 1 + 2 * f)
                    load(1, w3v[:, :, bass.ds(f * P, P)], u0 + 2 + 2 * f)
                with sp.Fori(0, NFF // 2) as k:
                    for j in range(2):
                        load(j, ffn_w2[0, bass.ds(k * 2 * P + j * P, P), :], u0 + NUP + 1 + j + 2 * k)
            for t in range(TT):
                sp.wait_ge(s_fin, t + 1)
                sp.dma_start(out[0, t * P:(t + 1) * P, :], x1[:, t, :]).then_inc(s_out, 16)
            sp.wait_ge(s_out, 16 * TT)

        @block.gpsimd
        def _(pool):
            pool.sem_inc(s_flo, 2)

            def low(slot, after):
                pool.wait_ge(s_fhi, after)
                pool.tensor_tensor(fw_lo[:, slot, :], fw_raw[:, slot, :], fw_hi[:, slot, :].bitcast(F32), ALU.subtract)\
                    .then_inc(s_flo, 1)

            for half in range(2):
                u0 = half * NUNITS
                with pool.Fori(0, NFF) as f:
                    low(0, u0 + 1 + 2 * f)
                    low(1, u0 + 2 + 2 * f)
                with pool.Fori(0, NFF // 2) as k:
                    low(0, u0 + NUP + 1 + 2 * k)
                    low(1, u0 + NUP + 2 + 2 * k)

        @block.tensor
        def _(pe):
            pe.sem_inc(s_fused, 2)
            for half in range(2):
                u0 = half * NUNITS
                for m in range(KT):
                    if half and m == 0:
                        pe.wait_ge(s_dn, 8)
                    if m >= 4:
                        pe.wait_ge(s_tre, KT * half + m - 3)
                    elif half:
                        pe.wait_ge(s_tre, KT)
                    for t in range(4):
                        last = pe.transpose(psum[4 + m % 4][:, t * P:(t + 1) * P], x1[:, 4 * half + t, m * P:(m + 1) * P],
                                            ident[:, :])
                    last.then_inc(s_tr, 1)
                pe.wait_ge(s_h2, KT * (half + 1))
                with pe.Fori(0, NFF // 2) as i:
                    for par in range(2):
                        pe.wait_ge(s_ff, NFF * half + 1 + par + 2 * i)
                        for b in range(2):
                            u = 2 * par + b
                            pe.wait_ge(s_flo, u0 + 3 + u + 4 * i)
                            w_h, w_l = kcols(fw_hi[:, b, :]), kcols(fw_lo[:, b, :])
                            for k in range(KT):
                                last = split3(pe, psum[2 * par + b][:, :], w_h[:, k, :], w_l[:, k, :], h2_hi[:, k, :],
                                              h2_lo[:, k, :], k == 0, k == KT - 1)
                            last.then_inc(s_fused, 1)
                pe.wait_ge(s_ff, NFF * (half + 1) + 2)
                pe.wait_ge(s_tre, KT * (half + 1))
                for k in range(NFF):
                    pe.wait_ge(s_flo, u0 + NUP + 3 + k)
                    for t in range(4):
                        for nb in range(2):
                            cs = slice(512 * nb, 512 * nb + 512)
                            last = split3(pe, psum[2 * t + nb][:, :], ff_hi[:, k, t * P:(t + 1) * P],
                                          ff_lo[:, k, t * P:(t + 1) * P], fw_hi[:, k % 2, cs], fw_lo[:, k % 2, cs],
                                          k == 0, k == NFF - 1)
                    last.then_inc(s_fused, 1)

        @block.scalar
        def _(act):
            def take(slot, loaded, used):
                act.wait_ge(s_fraw[slot], loaded)
                act.wait_ge(s_fused, used)
                act.activation(fw_hi[:, slot, :], fw_raw[:, slot, :], ACT.Copy).then_inc(s_fhi, 1)

            def norm(half):
                for pr in range(2):
                    t = slice(4 * half + 2 * pr, 4 * half + 2 * pr + 2)
                    n = 2 * half + pr
                    act.wait_ge(s_mv2, n + 1)
                    act.activation(rstd2[:, t, 0:1], mv2[:, t, 1:2], ACT.Ln, bias=eps[:, 0:1]).then_inc(s_ln2, 1)
                    act.wait_ge(s_ln2, 2 * n + 1)
                    act.activation(rstd2[:, t, 0:1], rstd2[:, t, 0:1], ACT.Exp, scale=-0.5).then_inc(s_ln2, 1)
                    act.wait_ge(s_rstd2, n + 1)
                    for i in range(4 * half + 2 * pr, 4 * half + 2 * pr + 2):
                        act.activation(x1[:, i, :], x1[:, i, :], ACT.Identity, scale=rstd2[:, i, 0:1], bias=rstd2[:, i, 1:2])\
                           .then_inc(s_xn2, 1)

            for half in range(2):
                u0 = half * NUNITS
                n0 = u0 // 2
                for b in range(2):
                    take(b, 16 * (n0 + 1), u0 + 1 + b)
                if half:
                    act.wait_ge(s_mv2, 2)
                for m in range(KT):
                    act.wait_ge(s_tr, KT * half + m + 1)
                    if m >= 2:
                        act.wait_ge(s_h2, KT * half + m - 1)
                    act.activation(ft[:, m % 2, :], psum[4 + m % 4][:, :], ACT.Identity, scale=hcol[:, 0, m:m + 1],
                                   bias=hcol[:, 1, m:m + 1]).then_inc(s_tre, 1)
                if half:
                    act.wait_ge(s_res, TT)
                    act.dma_start(ln1g[:, :], ln2_g.to_broadcast([P, DM])).then_inc(s_lnp2, 16)
                    act.dma_start(ln1b[:, :], ln2_b.to_broadcast([P, DM])).then_inc(s_lnp2, 16)
                    norm(0)
                act.wait_ge(s_h2, KT * (half + 1))
                with act.Fori(0, NFF // 2) as i:
                    for par in range(2):
                        take(0, 16 * (n0 + 2 + par) + 32 * i, u0 + 3 + 2 * par + 4 * i)
                        act.wait_ge(s_ff, NFF * half + 1 + par + 2 * i)
                        act.activation(ft[:, par, :], psum[2 * par][:, :], ACT.Silu).then_inc(s_silu2, 1)
                        take(1, 16 * (n0 + 2 + par) + 32 * i, u0 + 4 + 2 * par + 4 * i)
                with act.Fori(1, NFF // 2) as k:
                    for b in range(2):
                        take(b, 16 * (n0 + NFF + 1) + 16 * k, u0 + NUP + 1 + b + 2 * k)
            norm(1)

        @block.vector
        def _(dve):
            dve.sem_inc(s_ff, 2)
            own = Chain(dve, ch5["dve"])

            def down(half):
                dve.wait_ge(s_fused, NUNITS * (half + 1) + 2)
                for t in range(4):
                    i = 4 * half + t
                    for nb in range(2):
                        cs = slice(512 * nb, 512 * nb + 512)
                        n = 8 * half + 2 * t + nb
                        dve.tensor_tensor(ft[:, nb, :], psum[2 * t + nb][:, :], gate2[:, cs], ALU.mult).then_inc(s_dn, 1)
                        dve.wait_ge(s_dn, n + 1)
                        own.seq(dve.scalar_tensor_tensor(x1[:, i, cs], x1[:, i, cs], ALPHA, ft[:, nb, :], ALU.mult, ALU.add))
                        own.tick(dve.bn_stats(stat2[:, t % 2, 6 * nb:6 * nb + 6], x1[:, i, cs]))
                    own.wait()
                    ins = dve.bn_aggr(mv2[:, i, :], stat2[:, t % 2, :])
                    if t % 2:
                        ins.then_inc(s_mv2, 1)
                    else:
                        own.seq(ins)

            def nmr(half):
                for pr in range(2):
                    n = 2 * half + pr
                    t = slice(2 * n, 2 * n + 2)
                    dve.wait_ge(s_ln2, 2 * n + 2)
                    dve.scalar_tensor_tensor(rstd2[:, t, 1:2], mv2[:, t, 0:1], -1.0, rstd2[:, t, 0:1], ALU.mult, ALU.mult)\
                       .then_inc(s_rstd2, 1)

            def affine(half):
                dve.wait_ge(s_lnp2, 32)
                for i in range(4 * half, 4 * half + 4):
                    dve.wait_ge(s_xn2, i + 1)
                    own.seq(dve.tensor_tensor(x1[:, i, :], x1[:, i, :], ln1g[:, :], ALU.mult))
                    dve.tensor_tensor(x1[:, i, :], x1[:, i, :], ln1b[:, :], ALU.add).then_inc(s_fin, 1)

            for half in range(2):
                u0 = half * NUNITS
                if half:
                    down(0)
                for m in range(KT):
                    dve.wait_ge(s_tre, KT * half + m + 1)
                    own.seq(dve.tensor_copy(h2_hi[:, m, :], ft[:, m % 2, :]))
                    dve.tensor_tensor(h2_lo[:, m, :], ft[:, m % 2, :], h2_hi[:, m, :].bitcast(F32), ALU.subtract).then_inc(s_h2, 1)
                dve.wait_ge(s_lnp, 32)
                for i in range(4 * half, 4 * half + 4):
                    own.seq(dve.tensor_tensor(x1[:, i, :], x1[:, i, :], ln1g[:, :], ALU.mult))
                    dve.tensor_tensor(x1[:, i, :], x1[:, i, :], ln1b[:, :], ALU.add).then_inc(s_res, 1)
                if half:
                    nmr(0)
                    affine(0)
                else:
                    dve.wait_ge(s_res, 4)
                with dve.Fori(0, NFF // 2) as i:
                    for par in range(2):
                        f = 2 * i + par
                        done = NFF * half + 1 + par + 2 * i
                        dve.wait_ge(s_silu2, done)
                        dve.wait_ge(s_fused, u0 + 4 + 2 * par + 4 * i)
                        t = ft[:, par, :]
                        dve.tensor_tensor(t, t, psum[2 * par + 1][:, :], ALU.mult).then_inc(s_prod, 1)
                        dve.wait_ge(s_prod, done)
                        dve.tensor_copy(ff_hi[:, f, :], t).then_inc(s_ffhi, 1)
                        dve.wait_ge(s_ffhi, done)
                        dve.tensor_tensor(ff_lo[:, f, :], t, ff_hi[:, f, :].bitcast(F32), ALU.subtract).then_inc(s_ff, 1)
            down(1)
            nmr(1)
            affine(1)


_INS = ["x", "c", "w_ada", "b_ada", "w_in", "hg_lb_logits", "hg_norm_g", "cmp_pos_k", "cmp_w1_k", "cmp_w2_k",
        "cmp_pos_v", "cmp_w1_v", "cmp_w2_v", "w_out", "ln1_g", "ln1_b", "ffn_w1", "ffn_w3", "ffn_w2", "ln2_g", "ln2_b"]


def kernel(**inputs):
    import numpy as _np
    import concourse.bacc as _bacc
    from concourse import mybir as _mybir
    from concourse.bass_utils import run_bass_kernel_spmd as _run

    nc = _bacc.Bacc("TRN2", target_bir_lowering=False, num_devices=1)
    arrays, args = {}, []
    for name in _INS:
        a = _np.ascontiguousarray(inputs[name])
        arrays[f"in_{name}_dram"] = a
        args.append(nc.dram_tensor(f"in_{name}_dram", a.shape, _mybir.dt.from_np(a.dtype), kind="ExternalInput").ap())
    args.append(nc.dram_tensor("out_0_dram", (1, SEQ, DM), F32, kind="ExternalOutput").ap())
    program(nc, *args)
    r = _run(nc, [arrays], core_ids=[0])
    return r.results[0]["out_0_dram"]
```

```python
import concourse.bass as bass
from concourse import mybir
import numpy as np

F32, F32R, BF16, I8 = mybir.dt.float32, mybir.dt.float32r, mybir.dt.bfloat16, mybir.dt.int8
ALU = mybir.AluOpType
ACT = mybir.ActivationFunctionType
AX = mybir.AxisListType

P = 128
SEQ, DM = 1024, 1024
KT = DM // P
TT = SEQ // P
HEADS, DH, GROUPS, HG = 8, 64, 2, 4
CMP_STRIDE, CMP_BLOCK, NCMP, CMP_HID = 16, 32, 63, 256
D_FF = 2816
NFF = D_FF // P
WINDOW = 512
ALPHA = 2.0 ** 0.25
LN_EPS, RMS_EPS = 1e-5, 1e-6
NEG = -1e30
FLOOR = 1e29
SLOPES = [2.0 ** -(h + 1) for h in range(HEADS)]
IN_COLS = 3352
C_Q, C_F, C_V, C_G, C_NQ, C_KC, C_VC, C_KS, C_VS, C_KW, C_VW = (
    0, 512, 1024, 1536, 2048, 2560, 2688, 2816, 2944, 3072, 3200)
NGATE = 3 * HEADS
UW = P + NGATE


class Map:

    def __init__(self, nc, base, limit):
        self.nc, self.at, self.limit = nc, (base + 63) // 64 * 64, limit

    def __call__(self, name, shape, dtype=F32):
        size = int(np.prod(shape[1:])) * {F32: 4, F32R: 4, BF16: 2, I8: 1}[dtype]
        t = self.nc.alloc_sbuf_tensor_at(name, shape, dtype, offset=self.at)
        self.at = (self.at + size + 63) // 64 * 64
        assert self.at <= self.limit, (name, self.at, self.limit)
        return t

    def rest(self):
        return Map(self.nc, self.at, self.limit)


class Banks:

    def __init__(self, nc, psum, tag):
        self.psum = psum
        self.filled = [nc.alloc_semaphore(f"{tag}_filled{b}") for b in range(8)]
        self.emptied = [nc.alloc_semaphore(f"{tag}_emptied{b}") for b in range(8)]
        self.turns, self.of, self.next = [0] * 8, {}, {}

    def plan(self, pool, *key):
        i = self.next.get(pool, 0)
        self.next[pool] = i + 1
        b = pool[i % len(pool)]
        self.turns[b] += 1
        self.of[key] = (b, self.turns[b])

    def tile(self, *key):
        return self.psum[self.of[key][0]]

    def begin(self, pe, *key):
        b, n = self.of[key]
        if n > 1:
            pe.wait_ge(self.emptied[b], n - 1)
        return self.psum[b]

    def fill(self, ins, *key):
        ins.then_inc(self.filled[self.of[key][0]], 1)

    def wait_filled(self, eng, *key):
        b, n = self.of[key]
        eng.wait_ge(self.filled[b], n)
        return self.psum[b]

    def empty(self, ins, *key):
        ins.then_inc(self.emptied[self.of[key][0]], 1)

    def wait_emptied(self, eng, *key):
        b, n = self.of[key]
        eng.wait_ge(self.emptied[b], n)


class Chain:

    def __init__(self, eng, sem):
        self.eng, self.sem, self.n = eng, sem, 0

    def tick(self, ins):
        self.n += 1
        ins.then_inc(self.sem, 1)

    def wait(self):
        self.eng.wait_ge(self.sem, self.n)

    def seq(self, ins):
        self.tick(ins)
        self.wait()


def split3(pe, out, a_hi, a_lo, b_hi, b_lo, first, last):
    pe.matmul(out, a_hi, b_hi, start=first, stop=False, skip_group_check=True)
    pe.matmul(out, a_hi, b_lo, start=False, stop=False, skip_group_check=True)
    return pe.matmul(out, a_lo, b_hi, start=False, stop=last, skip_group_check=True)


def program(nc, x, c, w_ada, b_ada, w_in, hg_lb_logits, hg_norm_g, cmp_pos_k, cmp_w1_k, cmp_w2_k,
            cmp_pos_v, cmp_w1_v, cmp_w2_v, w_out, ln1_g, ln1_b, ffn_w1, ffn_w3, ffn_w2, ln2_g, ln2_b, out):
    sem = nc.alloc_semaphore
    psum = [nc.alloc_psum_tensor(f"bank{b}", [P, 512], F32) for b in range(8)]
    top = Map(nc, nc.sbuf_base, nc.sbuf_usable_end)

    ident = top("ident", [P, P])
    ident_bf = top("ident_bf", [P, P], BF16)
    ones = top("ones", [P, P])
    causal_q = top("causal_q", [P, P], BF16)
    causal_k = top("causal_k", [P, P], BF16)
    edge_q = top("edge_q", [P, P], BF16)
    edge_k = top("edge_k", [P, P], BF16)
    cmp_q = top("cmp_q", [P, TT, 64], BF16)
    cmp_k = top("cmp_k", [64, SEQ], BF16)
    cols = top("cols", [P, 108])
    ada = top("ada", [P, 4, KT])
    lb = top("lb", [P, 4])
    oml = top("oml", [P, 4])
    eps = top("eps", [P, 2])
    silu_c = top("silu_c", [P, KT])
    row_of = top("row_of", [71, 3])
    kc_a = top("kc_a", [P, GROUPS, 64], F32R)
    kc_b = top("kc_b", [71, GROUPS, 64], F32R)
    vc_sb = top("vc_sb", [64, GROUPS, 65])
    hcol = top("hcol", [P, 2, KT])
    mix_h_at = top.at
    mix_h = top("mix_h", [P, HG, SEQ])
    hd = [None, None]
    hd_at = top.at
    hd[0] = [top("hd0_f", [P, SEQ]), top("hd0_q", [P, SEQ]), top("hd0_v", [P, TT, P]), top("hd0_g", [P, TT * UW])]
    body = top

    A = body.rest()
    w_raw = A("w_raw", [P, 2, KT, UW])
    w_hi = A("w_hi", [P, 2, KT, UW], F32R)
    w_lo = A("w_lo", [P, 2, KT, UW], F32R)
    R1 = A.rest()
    hgm = A("hgm", [P, 8, P], I8)
    reset = A("reset", [P, SEQ], BF16)
    hd[1] = [A("hd1_f", [P, SEQ]), A("hd1_q", [P, SEQ]), A("hd1_v", [P, TT, P]), A("hd1_g", [P, SEQ])]
    hb = A("hb", [P, SEQ])
    hk = A("hk", [P, SEQ])
    hD = A("hD", [P, 2, SEQ])
    hW = A("hW", [P, 2, SEQ])
    hQb = A("hQb", [P, SEQ])
    hKT = A("hKT", [P, TT, P])
    hS = A("hS", [P, TT, P])
    hAT = A("hAT", [P, 2, 4, P])
    heb = A("heb", [P, TT])
    ho = A("ho", [P, 2, 512])
    ho2 = A("ho2", [P, 2, 512])
    vst = A("vst", [P, SEQ])
    hT_at = A.at
    hT_hi = A("hT_hi", [P, KT, SEQ], F32R)
    hT_lo = A("hT_lo", [P, KT, SEQ], F32R)
    E = R1.rest()
    hgm_room = E("hgm_room", [P, 3 * SEQ // 4])
    x_sb = E("x_sb", [P, TT, DM])
    wa = E("wa", [P, KT, 512])
    prm = E("prm", [108, P])
    acc = E("acc", [P, 512])
    h32 = E("h32", [P, 2, 512])
    E.limit = hT_at
    Cm = R1.rest()
    Cm("hgm_room2", [P, 3 * SEQ // 4])
    a2 = Cm("a2", [P, 2, GROUPS, SEQ])
    w1c = Cm("w1c", [P, 2, 16, CMP_HID])
    w2c = Cm("w2c", [P, 2, 2, DH])
    zc = Cm("zc", [P, 2, 2, 2 * GROUPS * NCMP])
    zb = Cm("zb", [P, 2, 2])
    zacc = Cm("zacc", [P, 2, CMP_HID])
    kst_c = Cm("kst_c", [71, GROUPS, 64])
    assert Cm.at <= hT_at
    B = R1.rest()
    nq = B("nq", [P, 4, SEQ])
    mix_n_at = B.at
    mix_n = B("mix_n", [P, 4, SEQ])
    hold = Map(nc, nc.sbuf_usable_end - 10 * DM * 4 - 64, nc.sbuf_usable_end)
    x1_at = hold.at
    x1 = hold("x1", [P, TT, DM])
    B.limit = hold.at
    gate1 = hold("gate1", [P, DM])
    gate2 = hold("gate2", [P, DM])
    ka_a = B("ka_a", [P, 2, GROUPS, SEQ], F32R)
    ka_b = B("ka_b", [71, 2, GROUPS, SEQ], F32R)
    kp = B("kp", [65, 2, GROUPS, SEQ], F32R)
    kst = [B("kst_s", [71, SEQ]), B("kst_w", [71, SEQ])]
    va = B("va", [P, 2, TT, GROUPS, DH + 1])
    gates = B("gates", [P, TT, NGATE])
    wa2 = B("wa2", [P, 2, KT // 2, 512])
    brow = B("brow", [1, 2 * DM])
    Bl = body.rest()
    Bl.limit = R1.at
    qst = Bl("qst", [DH, HG, P])
    q_a = Bl("q_a", [P, 4, HG * P], F32R)
    q_b = Bl("q_b", [71, 4, HG * P], F32R)
    pt = Bl("pt", [P, 4, HG * P])
    acc2 = Bl("acc2", [P, 512])
    yb = B("yb", [P, 2, 2, HG * DH])
    ot = B("ot", [DH + 1, 2, HG * P])
    mx = B("mx", [P, HG, 3])
    negm = B("negm", [P, 2, HG, 7])
    pm = B("pm", [P, HG, 4])
    rc = B("rc", [P, 3, HG])
    C1 = Map(nc, hd_at, mix_n_at)
    wo_raw = C1("wo_raw", [P, 2, KT, 256])
    wo_hi = C1("wo_hi", [P, 2, KT, 256], F32R)
    wo_lo = C1("wo_lo", [P, 2, KT, 256], F32R)
    wt = C1("wt", [P, 2, 512])
    stat = C1("stat", [P, 2, 12])
    mv = C1("mv", [P, TT, 2])
    rstd = C1("rstd", [P, TT, 2])
    C2 = Map(nc, mix_n_at + 4 * SEQ * 4, x1_at)
    mix_hi = C2("mix_hi", [P, KT, SEQ], F32R)
    mix_lo = C2("mix_lo", [P, KT, SEQ], F32R)
    D = Map(nc, mix_h_at, x1_at)
    fw_raw = D("fw_raw", [P, 2, DM])
    ln1g = D("ln1g", [P, DM])
    ln1b = D("ln1b", [P, DM])
    h2_hi = D("h2_hi", [P, KT, 512], F32R)
    h2_lo = D("h2_lo", [P, KT, 512], F32R)
    gated_at = D.at + (NFF - 8) * 512 * 4
    ff_hi = D("ff_hi", [P, NFF, 512], F32R)
    gated = Map(nc, gated_at, D.at)("gated", [P, 8, 512])
    ff_lo = D("ff_lo", [P, NFF, 512], F32R)
    fw_hi = D("fw_hi", [P, 2, DM], F32R)
    fw_lo = D("fw_lo", [P, 2, DM], F32R)
    ft = D("ft", [P, 2, 512])
    stat2 = D("stat2", [P, 2, 12])
    mv2 = D("mv2", [P, TT, 2])
    rstd2 = D("rstd2", [P, TT, 2])

    bk = Banks(nc, psum, "a")
    bk.plan((7,), "prm")
    for v in range(4):
        bk.plan((7,), "ada", v)
    for m in range(KT):
        for half in range(2):
            bk.plan((0, 1, 2, 3), "xt", m, half)

    consts = sem("consts")
    s_prm, s_c, s_x = sem("prm_loaded"), sem("c_loaded"), [sem("x_loaded0"), sem("x_loaded1")]
    s_wa = [sem(f"ada_weights_loaded{q}") for q in range(4)]
    s_acc = sem("ada_products_summed")
    s_cols, s_hT = sem("lower_bound_ready"), sem("h_split")
    s_silu = sem("silu_c_ready")
    ch = {e: sem(f"{e}_chain") for e in ("act", "dve", "pool")}
    s_out = sem("out_stored")

    units = [(True, C_KC, P), (True, C_VC, P)]
    for h in range(HG):
        units += [(True, C_F + h * P, P), (True, C_Q + h * P, P), (True, C_V + h * P, P), (True, C_G + h * P, P)]
    units += [(True, C_KS, P), (True, C_KW, P), (True, C_VS, P), (False, C_VW, UW)]
    units += [(True, C_NQ + j * P, P) for j in range(4)]
    wd = w_in[0].rearrange("(k p) n -> p k n", p=P)
    s_wraw, s_whi, s_wlo = [sem("w_raw_loaded0"), sem("w_raw_loaded1")], sem("w_hi_ready"), sem("w_lo_ready")

    wada_v = w_ada[0].rearrange("(p k) n -> p k n", k=KT)
    ADA = [(1, 0), (1, 1), (0, 0), (0, 1)]

    with nc.Block() as block:
        @block.sync
        def _(sp):
            sp.dma_start(prm[0:48, :], b_ada[0].rearrange("(m p) -> m p", p=P)).then_inc(s_prm, 16)
            sp.dma_start(prm[48:52, :], hg_norm_g[0].rearrange("(m p) -> m p", p=P)).then_inc(s_prm, 16)
            sp.dma_start(prm[52:60, :], hg_lb_logits.rearrange("a (m p) -> (a m) p", p=P)).then_inc(s_prm, 16)
            sp.dma_start(prm[60:76, :], cmp_pos_k[0].rearrange("(m a) d -> m (a d)", a=2)).then_inc(s_prm, 16)
            sp.dma_start(prm[76:92, :], cmp_pos_v[0].rearrange("(m a) d -> m (a d)", a=2)).then_inc(s_prm, 16)
            sp.dma_start(prm[92:100, :], ln1_g[0].rearrange("(m p) -> m p", p=P)).then_inc(s_prm, 16)
            sp.dma_start(prm[100:108, :], ln1_b[0].rearrange("(m p) -> m p", p=P)).then_inc(s_prm, 16)
            sp.dma_start(silu_c[:, :], c[0].rearrange("(p k) -> p k", k=KT)).then_inc(s_c, 16)
            for v, (vec, half) in enumerate(ADA):
                at = vec * DM + half * 512
                for q in range(4):
                    if v:
                        sp.wait_ge(s_acc, 4 * v - 3 + q)
                    sp.dma_start(wa[:, 2 * q:2 * q + 2, :], wada_v[:, 2 * q:2 * q + 2, at:at + 512]).then_inc(s_wa[q], 16)
            for v in range(2):
                sp.dma_start(x_sb[:, 4 * v:4 * v + 4, :],
                             x[0, 512 * v:512 * v + 512, :].rearrange("(t p) d -> p t d", p=P)).then_inc(s_x[v], 16)
            for u in range(2):
                sp.dma_start(w_raw[:, u, :, 0:P], wd[:, :, units[u][1]:units[u][1] + P]).then_inc(s_wraw[u], 16)

        @block.gpsimd
        def _(pool):
            own = Chain(pool, ch["pool"])
            own.seq(pool.memset(ident[:, :], 0.0))
            own.seq(pool.affine_select(out=ident[:, :], in_=ident[:, :], compare_op=ALU.not_equal, fill=1.0,
                                       base=0, pattern=[[-1, P]], channel_multiplier=1))
            pool.memset(ones[:, :], 1.0)
            own.seq(pool.memset(eps[:, 0:1], LN_EPS))
            own.seq(pool.memset(eps[:, 1:2], RMS_EPS))
            pool.tensor_copy(ident_bf[:, :], ident[:, :]).then_inc(consts, 1)
            for m in (causal_q, causal_k, edge_q, edge_k, cmp_q, cmp_k):
                own.tick(pool.memset(m[:], 0.0))
            own.tick(pool.memset(reset[:, :], 1.0))
            own.tick(pool.memset(hgm[:, :, :], 0.0))
            own.wait()
            own.seq(pool.memset(row_of[64:71, :], 0.0))
            for col, row in ((0, 0), (1, 2), (1, 5), (2, 3), (2, 6)):
                own.seq(pool.affine_select(out=row_of[64:71, col:col + 1], in_=row_of[64:71, col:col + 1],
                                           compare_op=ALU.not_equal, fill=1.0, base=-row, pattern=[[0, 1]],
                                           channel_multiplier=1))

            def mask(m, base, pattern, mult):
                own.tick(pool.affine_select(out=m, in_=m, compare_op=ALU.is_ge, fill=NEG, base=base,
                                            pattern=pattern, channel_multiplier=mult))
            mask(causal_q[:, :], 0, [[-1, P]], 1)
            mask(causal_k[:, :], 0, [[1, P]], -1)
            mask(edge_q[:, :], -1, [[1, P]], -1)
            mask(edge_k[:, :], -1, [[-1, P]], 1)
            mask(cmp_q[:, :, :], 1 - CMP_BLOCK, [[P, TT], [-CMP_STRIDE, 64]], 1)
            mask(cmp_k[:, :], 1 - CMP_BLOCK, [[1, SEQ]], -CMP_STRIDE)
            own.tick(pool.memset(reset[:, :].rearrange("p (c t) -> p c t", t=P)[:, :, 0:1], 0.0))
            for i in range(7):
                L = 64 >> i
                up = hgm[:, i, :].rearrange("p (n u l) -> p n u l", u=2, l=L)[:, :, 1, :]
                nb = P // (2 * L)
                own.seq(pool.memset(up, 1.0))
                own.seq(pool.affine_select(out=up, in_=up, compare_op=ALU.is_ge, fill=0.0, base=0,
                                           pattern=[[-2 * L, nb], [0, L]], channel_multiplier=1))
                own.seq(pool.affine_select(out=up, in_=up, compare_op=ALU.is_ge, fill=0.0, base=L - 1,
                                           pattern=[[2 * L, nb], [0, L]], channel_multiplier=-1))
            own.seq(pool.tensor_copy(hgm[:, 7, :], ident[:, :]))
            for u in range(2):
                pool.wait_ge(s_whi, u + 1)
                pool.tensor_tensor(w_lo[:, u, :, 0:P], w_raw[:, u, :, 0:P], w_hi[:, u, :, 0:P].bitcast(F32),
                                   ALU.subtract).then_inc(s_wlo, 1)

        @block.vector
        def _(dve):
            own = Chain(dve, ch["dve"])
            ps = bk.wait_filled(dve, "prm")
            bk.empty(dve.tensor_copy(cols[:, :], ps[:, 0:108]), "prm")
            bk.wait_emptied(dve, "prm")
            own.seq(dve.tensor_tensor(oml[:, :], cols[:, 52:56], cols[:, 56:60], ALU.subtract))
            dve.wait_ge(s_cols, 1)
            own.seq(dve.tensor_scalar(oml[:, :], lb[:, :], -1.0, 1.0, ALU.mult, ALU.add))
            dve.wait_ge(s_silu, 1)
            for v, (vec, half) in enumerate(ADA):
                dve.wait_ge(s_wa[0], 16 * (v + 1))
                if v:
                    bk.wait_filled(dve, "ada", v - 1)
                own.seq(dve.tensor_scalar(acc[:, :], wa[:, 0, :], silu_c[:, 0:1], None, ALU.mult))
                for k in range(1, KT):
                    q, odd = divmod(k, 2)
                    if not odd:
                        dve.wait_ge(s_wa[q], 16 * (v + 1))
                    i = dve.scalar_tensor_tensor(acc[:, :], wa[:, k, :], silu_c[:, k:k + 1], acc[:, :], ALU.mult, ALU.add)
                    if odd:
                        i.then_inc(s_acc, 1)
                        dve.wait_ge(s_acc, 4 * v + q + 1)
                    else:
                        own.seq(i)
                ps = bk.wait_filled(dve, "ada", v)
                bk.empty(dve.scalar_tensor_tensor(ada[:, vec, 4 * half:4 * half + 4], ps[:, 0:4],
                                                  1.0 if vec == 1 else 0.0, cols[:, 8 * vec + 4 * half:8 * vec + 4 * half + 4],
                                                  ALU.add, ALU.add), "ada", v)
            for n in range(2 * KT):
                m, half = n // 2, n % 2
                bk.wait_emptied(dve, "xt", m, half)
                hi = hT_hi[:, m, 512 * half:512 * half + 512]
                own.seq(dve.tensor_copy(hi, h32[:, n % 2, :]))
                dve.tensor_tensor(hT_lo[:, m, 512 * half:512 * half + 512], h32[:, n % 2, :], hi.bitcast(F32),
                                  ALU.subtract).then_inc(s_hT, 1)

        @block.scalar
        def _(act):
            act.wait_ge(s_c, 16)
            act.activation(silu_c[:, :], silu_c[:, :], ACT.Silu).then_inc(s_silu, 1)
            act.wait_ge(ch["dve"], 1)
            act.activation(lb[:, :], oml[:, :], ACT.Sigmoid).then_inc(s_cols, 1)
            bk.wait_emptied(act, "ada", 3)
            for n in range(2 * KT):
                m, half = n // 2, n % 2
                if n >= 2:
                    act.wait_ge(s_hT, n - 1)
                ps = bk.wait_filled(act, "xt", m, half)
                bk.empty(act.activation(h32[:, n % 2, :], ps[:, :], ACT.Identity, bias=ada[:, 0, m:m + 1],
                                        scale=ada[:, 1, m:m + 1]), "xt", m, half)
            for u in range(2):
                act.wait_ge(s_wraw[u], 16)
                act.activation(w_hi[:, u, :, 0:P], w_raw[:, u, :, 0:P], ACT.Copy).then_inc(s_whi, 1)

        @block.tensor
        def _(pe):
            pe.wait_ge(consts, 1)
            pe.wait_ge(s_prm, 112)
            bk.fill(pe.transpose(bk.begin(pe, "prm")[:, 0:108], prm[:, :], ident[0:108, 0:108]), "prm")
            for v in range(4):
                pe.wait_ge(s_acc, 4 * v + 4)
                ps = bk.begin(pe, "ada", v)
                for j in range(4):
                    i = pe.matmul(ps[:, j:j + 1], acc[:, j * P:(j + 1) * P], ones[:, 0:1], start=True, stop=True)
                bk.fill(i, "ada", v)
            for m in range(KT):
                for half in range(2):
                    pe.wait_ge(s_x[half], 16)
                    ps = bk.begin(pe, "xt", m, half)
                    for t in range(4):
                        i = pe.transpose(ps[:, t * P:(t + 1) * P], x_sb[:, 4 * half + t, m * P:(m + 1) * P], ident[:, :])
                    bk.fill(i, "xt", m, half)

    NU = len(units)
    U_KV, U_NQ = 2 + 4 * HG, 6 + 4 * HG
    def turns(u):
        fm, _, width = units[u]
        return 2 if fm or width == P else 4

    order = []
    for u in range(6):
        order.append(("unit", u))
        if u in (2, 3):
            order.append(("pos", u - 2))
        if u == 3:
            order.append(("cz", 0))
        if u == 4:
            order += [("cz", 1), ("gelu", 0)]
        if u == 5:
            order += [("gelu", 1), ("ckv",), ("vt", 4)]
    for h in range(HG):
        n = 6 + 4 * h
        if h == 0:
            order.append(("prep", 0))
        order += [("ew", h, 0), ("ew", h, 1), ("unit", n), ("kt", h), ("ew", h, 2), ("us", h),
                  ("ew", h, 3), ("gram", h, 2), ("unit", n + 1), ("ew", h, 4), ("gram", h, 3), ("ew", h, 5),
                  ("gram", h, 4), ("unit", n + 2), ("ew", h, 6), ("gram", h, 5), ("ew", h, 7), ("gram", h, 6),
                  ("unit", n + 3), ("ew", h, 8), ("gram", h, 7), ("gram", h, 8), ("vt", n + 2), ("gram", h, 9)]
        if h + 1 < HG:
            order.append(("prep", h + 1))
        else:
            order.append(("unit", U_NQ))
        order.append(("o", h))
    order += [("unit", u) for u in range(U_NQ + 1, NU)] + [("evac_last",)]

    LOW, HIGH = (0, 1, 2, 3), (4, 5, 6, 7)
    for step in order:
        kind, a = step[0], step[1:]
        if kind == "unit":
            for i in range(turns(a[0])):
                bk.plan(LOW, "u", a[0], i)
        elif kind == "cz":
            bk.plan(HIGH, "cz", a[0])
        elif kind == "vt":
            for b in range(2):
                bk.plan(HIGH, "vt", a[0], b)
        elif kind == "ckv":
            bk.plan(HIGH, "ck")
            bk.plan(HIGH, "cv")
        elif kind in ("kt", "us", "gram"):
            for b in range(2):
                bk.plan(HIGH, kind, *a, b)
        elif kind == "o":
            for b in range(2):
                bk.plan(HIGH, "o", a[0], b)
            for b in range(2):
                bk.plan(HIGH, "ss", a[0], b)

    s_w1 = [sem("cmp_weights_loaded0"), sem("cmp_weights_loaded1")]
    s_kst, s_tanh_in, s_tanh = sem("kst_rows_ready"), sem("tanh_argument_ready"), sem("tanh_ready")
    s_sigq = sem("q_sigmoid_ready")
    s_decay, s_ln = sem("decay_ready"), sem("log_decay_ready")
    s_diff, s_exp, s_w = sem("exponent_ready"), sem("exp_ready"), sem("factor_ready")
    s_state, s_sq, s_rs, s_y = sem("states_ready"), sem("squares_ready"), sem("rms_ready"), sem("y_hg_ready")
    s_zacc = sem("position_products_ready")
    s_mid, s_kc = sem("gelu_ready"), sem("cmp_keys_ready")

    ch2 = {e: sem(f"{e}_chain_b") for e in ("act", "dve", "pool")}

    def level_views(t, j):
        L = 64 >> (j - 2)
        v = t.rearrange("p (n u l) -> p n u l", u=2, l=L)
        return v[:, :, 0, :], v[:, :, 1, :]

    with nc.Block() as block:
        @block.sync
        def _(sp):
            for kv, (w1, w2) in enumerate(((cmp_w1_k, cmp_w2_k), (cmp_w1_v, cmp_w2_v))):
                sp.dma_start(w1c[:, kv, :, :], w1[0].rearrange("(c p) n -> p c n", p=P)).then_inc(s_w1[kv], 16)
                sp.dma_start(w2c[:, kv, :, :], w2[0].rearrange("(c p) n -> p c n", p=P)).then_inc(s_w1[kv], 16)
            for u in range(2, NU):
                _, col, width = units[u]
                sp.wait_ge(s_wlo, u - 1)
                sp.dma_start(w_raw[:, u % 2, :, 0:width], wd[:, :, col:col + width]).then_inc(s_wraw[u % 2], 16)

        @block.gpsimd
        def _(pool):
            own = Chain(pool, ch2["pool"])
            own.seq(pool.memset(kst_c[64:71, :, :], 0.0))
            for row in (1, 4):
                own.seq(pool.affine_select(out=kst_c[64:71, :, :], in_=kst_c[64:71, :, :], compare_op=ALU.not_equal,
                                           fill=1.0, base=-row, pattern=[[0, GROUPS], [0, 64]], channel_multiplier=1))
            pool.iota(kst_c[64:65, :, :], [[0, GROUPS], [CMP_STRIDE, 64]], base=CMP_BLOCK - 1, channel_multiplier=0,
                      allow_small_or_imprecise_dtypes=True).then_inc(s_kst, 1)
            pool.wait_ge(s_kst, 1)
            for u in range(2, NU):
                width = units[u][2]
                pool.wait_ge(s_whi, u + 1)
                pool.tensor_tensor(w_lo[:, u % 2, :, 0:width], w_raw[:, u % 2, :, 0:width],
                                   w_hi[:, u % 2, :, 0:width].bitcast(F32), ALU.subtract).then_inc(s_wlo, 1)

        @block.tensor
        def _(pe):
            def unit(u):
                fm, _, width = units[u]
                s = u % 2
                pe.wait_ge(s_wlo, u + 1)
                for i in range(turns(u)):
                    ps = bk.begin(pe, "u", u, i)
                    if fm:
                        t = slice(512 * i, 512 * i + 512)
                        for k in range(KT):
                            last = split3(pe, ps[:, :], w_hi[:, s, k, 0:P], w_lo[:, s, k, 0:P], hT_hi[:, k, t], hT_lo[:, k, t],
                                          k == 0, k == KT - 1)
                    else:
                        per = TT // turns(u)
                        for j in range(per):
                            tok = slice((per * i + j) * P, (per * i + j + 1) * P)
                            o = ps[:, j * width:(j + 1) * width]
                            for k in range(KT):
                                last = split3(pe, o, hT_hi[:, k, tok], hT_lo[:, k, tok], w_hi[:, s, k, 0:width],
                                              w_lo[:, s, k, 0:width], k == 0, k == KT - 1)
                    bk.fill(last, "u", u, i)

            def cz(kv):
                pe.wait_ge(s_w1[kv], 32)
                bk.wait_emptied(pe, "u", kv, 1)
                ps = bk.begin(pe, "cz", kv)
                for jt in range(2):
                    for cc in range(16):
                        pe.matmul(ps[:, jt * 126:jt * 126 + 126], w1c[:, kv, cc, jt * P:(jt + 1) * P],
                                  a2[:, kv, :, 2 * cc:2 * cc + CMP_STRIDE * (NCMP - 1) + 1:CMP_STRIDE],
                                  start=cc == 0, stop=cc == 15)
                pe.wait_ge(s_zacc, kv + 1)
                for jt in range(2):
                    last = pe.matmul(ps[:, 252 + jt:253 + jt], zacc[:, kv, jt * P:(jt + 1) * P], ones[:, 0:1],
                                     start=True, stop=True)
                bk.fill(last, "cz", kv)

            def ckv():
                pe.wait_ge(s_mid, 1)
                ps = bk.begin(pe, "ck")
                for jt in range(2):
                    last = pe.matmul(ps[0:64, 0:126], w2c[:, 0, jt, :], zc[:, 0, 0, jt * 126:jt * 126 + 126],
                                     start=jt == 0, stop=jt == 1)
                bk.fill(last, "ck")
                pe.wait_ge(s_mid, 2)
                ps = bk.begin(pe, "cv")
                for g in range(GROUPS):
                    for jt in range(2):
                        at = jt * 126 + g * NCMP
                        last = pe.matmul(ps[0:NCMP, g * DH:(g + 1) * DH], zc[:, 1, 0, at:at + NCMP], w2c[:, 1, jt, :],
                                         start=jt == 0, stop=jt == 1)
                bk.fill(last, "cv")

            def kt(h):
                pe.wait_ge(s_w, 9 * h + 2)
                for b in range(2):
                    ps = bk.begin(pe, "kt", h, b)
                    for j in range(4):
                        cc = 4 * b + j
                        last = pe.transpose(ps[:, j * P:(j + 1) * P], hW[:, 1, cc * P:(cc + 1) * P], ident[:, :])
                    bk.fill(last, "kt", h, b)

            def vt(u):
                for b in range(2):
                    bk.wait_emptied(pe, "u", u, b)
                    ps = bk.begin(pe, "vt", u, b)
                    for j in range(4):
                        last = pe.transpose(ps[:, j * P:(j + 1) * P], vst[:, (4 * b + j) * P:(4 * b + j + 1) * P], ident[:, :])
                    bk.fill(last, "vt", u, b)

            def us(h):
                bk.wait_emptied(pe, "vt", 4 + 4 * h, 1)
                for b in range(2):
                    bk.wait_emptied(pe, "kt", h, b)
                    ps = bk.begin(pe, "us", h, b)
                    for j in range(4 - b):
                        cc = 4 * b + j
                        last = pe.matmul(ps[:, j * P:(j + 1) * P], hKT[:, cc, :], hd[h % 2][2][:, cc, :], start=True, stop=True)
                    bk.fill(last, "us", h, b)

            def gram(h, j):
                if j <= 8:
                    pe.wait_ge(s_w, 9 * h + j + 1)
                for b in range(2):
                    ps = bk.begin(pe, "gram", h, j, b)
                    for i in range(4):
                        t = slice((4 * b + i) * P, (4 * b + i + 1) * P)
                        l, r = (hW[:, j % 2, t], hW[:, j % 2, t]) if j <= 8 else (hk[:, t], hd[h % 2][1][:, t])
                        last = pe.matmul(ps[:, i * P:(i + 1) * P], l, r, start=True, stop=True)
                    bk.fill(last, "gram", h, j, b)

            def o(h):
                pe.wait_ge(s_state, h + 1)
                v = hd[h % 2][2]
                for b in range(2):
                    bk.wait_emptied(pe, "gram", h, 9, b)
                    ps = bk.begin(pe, "o", h, b)
                    for i in range(4):
                        cc = 4 * b + i
                        last = pe.matmul(ps[:, i * P:(i + 1) * P], v[:, cc, :], hAT[:, b, i, :], start=True, stop=cc == 0)
                        if cc:
                            last = pe.matmul(ps[:, i * P:(i + 1) * P], hS[:, cc, :], hQb[:, cc * P:(cc + 1) * P],
                                             start=False, stop=True)
                    bk.fill(last, "o", h, b)
                for b in range(2):
                    bk.wait_emptied(pe, "o", h, b)
                    bk.fill(pe.matmul(bk.begin(pe, "ss", h, b)[:, :], ones[:, :], ho2[:, b, :], start=True, stop=True),
                            "ss", h, b)

            do = {"unit": unit, "cz": cz, "ckv": ckv, "vt": vt, "kt": kt, "us": us, "gram": gram, "o": o}
            for step in order:
                if step[0] in do:
                    do[step[0]](*step[1:])

        @block.scalar
        def _(act):
            own = Chain(act, ch2["act"])

            def take(u):
                width = units[u][2]
                act.wait_ge(s_wraw[u % 2], 16 * (u // 2 + 1))
                if u >= 2:
                    bk.wait_filled(act, "u", u - 2, turns(u - 2) - 1)
                act.activation(w_hi[:, u % 2, :, 0:width], w_raw[:, u % 2, :, 0:width], ACT.Copy).then_inc(s_whi, 1)

            def evac(u):
                if u < 2:
                    return
                h, r = divmod(u - 2, 4)
                if h < HG:
                    hf, hq, hv, hgate = hd[h % 2]
                    if h >= 2 and r == 0:
                        act.wait_ge(s_y, 2 * (h - 1))
                    if h == 1 and r == 0:
                        act.wait_ge(s_kc, 1)
                elif u == U_KV:
                    act.wait_ge(s_y, 2 * (HG - 1))
                elif u == U_NQ:
                    act.wait_ge(s_y, 2 * HG)
                for i in range(turns(u)):
                    ps = bk.wait_filled(act, "u", u, i)
                    t = slice(512 * i, 512 * i + 512)
                    if h < HG and r == 1:
                        act.activation(hq[:, t], ps[:, :], ACT.Sigmoid).then_inc(s_sigq, 1)
                        continue
                    if h < HG and r == 0:
                        ins = act.activation(hf[:, t], ps[:, :], ACT.Sigmoid)
                    elif h < HG and r == 2:
                        ins = act.activation(vst[:, t], ps[:, :], ACT.Copy)
                    elif h < HG:
                        ins = act.activation(hgate[:, t], ps[:, :], ACT.Sigmoid)
                    elif u in (U_KV, U_KV + 1):
                        ins = act.activation(hd[0][u - U_KV][:, t], ps[:, :], ACT.Copy)
                    elif u == U_KV + 2:
                        ins = act.activation(vst[:, t], ps[:, :], ACT.Copy)
                    elif u == U_KV + 3:
                        ins = act.activation(hd[0][3][:, 2 * i * UW:2 * (i + 1) * UW], ps[:, 0:2 * UW], ACT.Copy)
                    else:
                        ins = act.activation(nq[:, u - U_NQ, t], ps[:, :], ACT.Copy)
                    bk.empty(ins, "u", u, i)

            def vt(u):
                hv = hd[(u - 2) // 4 % 2][2]
                for b in range(2):
                    ps = bk.wait_filled(act, "vt", u, b)
                    bk.empty(act.activation(hv[:, 4 * b:4 * b + 4, :], ps[:, :].rearrange("p (a n) -> p a n", n=P), ACT.Copy),
                             "vt", u, b)

            def unit(u):
                if 2 <= u + 1 < NU:
                    take(u + 1)
                if u:
                    evac(u - 1)

            def gelu(kv):
                act.wait_ge(s_tanh_in, kv + 1)
                act.activation(zc[:, kv, 1, :], zc[:, kv, 1, :], ACT.Tanh, scale=0.7978845608028654).then_inc(s_tanh, 1)

            def prep(h):
                act.wait_ge(s_decay, h + 1)
                act.activation(hb[:, :], hd[h % 2][0][:, :], ACT.Ln).then_inc(s_ln, 1)

            def ew(h, j):
                n = 9 * h + j
                act.wait_ge(s_diff, n + 1)
                d = hD[:, n % 2, :]
                if j == 0:
                    b = hd[h % 2][0]
                    act.activation(heb[:, :], b[:, P - 1::P], ACT.Exp)
                    act.activation(d, b[:, :], ACT.Exp).then_inc(s_exp, 1)
                elif j == 1:
                    act.activation(d, d, ACT.Exp).then_inc(s_exp, 1)
                else:
                    low, up = level_views(d, j)
                    act.activation(low, low, ACT.Exp, scale=-1.0)
                    act.activation(up, up, ACT.Exp).then_inc(s_exp, 1)

            def kt(h):
                if h:
                    bk.wait_filled(act, "us", h - 1, 1)
                for b in range(2):
                    ps = bk.wait_filled(act, "kt", h, b)
                    bk.empty(act.activation(hKT[:, 4 * b:4 * b + 4, :], ps[:, :].rearrange("p (a n) -> p a n", n=P),
                                            ACT.Copy), "kt", h, b)

            def o(h):
                for b in range(2):
                    ps = bk.wait_filled(act, "o", h, b)
                    if h:
                        act.wait_ge(s_y, 2 * (h - 1) + b + 1)
                    act.activation(ho2[:, b, :], ps[:, :], ACT.Square)
                    bk.empty(act.activation(ho[:, b, :], ps[:, :], ACT.Copy), "o", h, b)
                for b in range(2):
                    ps = bk.wait_filled(act, "ss", h, b)
                    bk.empty(act.activation(ho2[:, b, :], ps[:, :], ACT.Ln, scale=1.0 / P, bias=eps[:, 1:2]), "ss", h, b)
                    bk.wait_emptied(act, "ss", h, b)
                    act.activation(ho2[:, b, :], ho2[:, b, :], ACT.Exp, scale=-0.5).then_inc(s_rs, 1)

            do = {"unit": unit, "vt": vt, "gelu": gelu, "prep": prep, "ew": ew, "kt": kt, "o": o,
                  "evac_last": lambda: evac(NU - 1)}
            for step in order:
                if step[0] in do:
                    do[step[0]](*step[1:])

        @block.vector
        def _(dve):
            own = Chain(dve, ch2["dve"])
            def evac(u):
                if u < 2:
                    for i in range(2):
                        ps = bk.wait_filled(dve, "u", u, i)
                        skip = 1 - i
                        for g in range(GROUPS):
                            rows = slice(g * DH, (g + 1) * DH)
                            dve.tensor_copy(a2[0:DH, u, g, 512 * i:512 * i + 512], ps[rows, :])
                            ins = dve.tensor_copy(a2[DH:P, u, g, 512 * i - 1 + skip:512 * i + 511], ps[rows, skip:512])
                        bk.empty(ins, "u", u, i)
                elif u < U_KV and (u - 2) % 4 == 1:
                    hq = hd[(u - 2) // 4 % 2][1]
                    for i in range(2):
                        bk.wait_filled(dve, "u", u, i)
                        dve.wait_ge(s_sigq, 2 * ((u - 2) // 4) + i + 1)
                        t = slice(512 * i, 512 * i + 512)
                        bk.empty(dve.tensor_tensor(hq[:, t], hq[:, t], bk.tile("u", u, i)[:, :], ALU.mult), "u", u, i)

            def unit(u):
                if u:
                    evac(u - 1)

            def pos(kv):
                dve.wait_ge(s_w1[kv], 32)
                z = zacc[:, kv, :]
                own.seq(dve.tensor_scalar(z, w1c[:, kv, 0, :], cols[:, 60 + 16 * kv:61 + 16 * kv], None, ALU.mult))
                for cc in range(1, 16):
                    ins = dve.scalar_tensor_tensor(z, w1c[:, kv, cc, :], cols[:, 60 + 16 * kv + cc:61 + 16 * kv + cc], z,
                                                   ALU.mult, ALU.add)
                    if cc < 15:
                        own.seq(ins)
                ins.then_inc(s_zacc, 1)

            def gelu(kv):
                ps = bk.wait_filled(dve, "cz", kv)
                z, w = zc[:, kv, 0, :], zc[:, kv, 1, :]
                own.seq(dve.tensor_copy(zb[:, kv, :], ps[:, 252:254]))
                for jt in range(2):
                    t = slice(126 * jt, 126 * jt + 126)
                    ins = dve.tensor_scalar(z[:, t], ps[:, t], zb[:, kv, jt:jt + 1], None, ALU.add)
                bk.empty(ins, "cz", kv)
                bk.wait_emptied(dve, "cz", kv)
                own.seq(dve.tensor_tensor(w, z, z, ALU.mult))
                own.seq(dve.tensor_scalar(w, w, 0.044715, 1.0, ALU.mult, ALU.add))
                dve.tensor_tensor(w, w, z, ALU.mult).then_inc(s_tanh_in, 1)
                dve.wait_ge(s_tanh, kv + 1)
                own.seq(dve.scalar_tensor_tensor(z, w, 1.0, z, ALU.add, ALU.mult))
                dve.tensor_scalar(z, z, 0.5, None, ALU.mult).then_inc(s_mid, 1)

            def ckv():
                dve.wait_ge(s_kst, 1)
                own.seq(dve.memset(kst_c[0:64, :, :], 0.0))
                own.seq(dve.memset(vc_sb[:, :, :], 0.0))
                own.tick(dve.memset(vc_sb[:, :, DH:DH + 1], 1.0))
                ps = bk.wait_filled(dve, "ck")
                bk.empty(dve.tensor_copy(kst_c[0:64, :, 0:NCMP], ps[0:64, 0:126].rearrange("p (g n) -> p g n", g=GROUPS)), "ck")
                ps = bk.wait_filled(dve, "cv")
                bk.empty(dve.tensor_copy(vc_sb[0:NCMP, :, 0:DH], ps[0:NCMP, 0:P].rearrange("p (g n) -> p g n", g=GROUPS)), "cv")
                bk.wait_emptied(dve, "cv")
                own.seq(dve.tensor_copy(kc_a[0:64, :, :], kst_c[0:64, :, :]))
                own.tick(dve.tensor_copy(kc_a[64:128, :, :], kc_a[0:64, :, :].bitcast(F32)))
                own.tick(dve.tensor_tensor(kc_b[0:64, :, :], kst_c[0:64, :, :], kc_a[0:64, :, :].bitcast(F32), ALU.subtract))
                own.seq(dve.tensor_copy(kc_b[64:71, :, :], kst_c[64:71, :, :]))
                dve.sem_inc(s_kc, 1)
                own.seq(dve.memset(hAT[:, :, :, :], 0.0))

            def prep(h):
                hf = hd[h % 2][0]
                u = 2 + 4 * h
                for i in range(2):
                    bk.wait_emptied(dve, "u", u, i)
                dve.tensor_scalar(hf[:, :], hf[:, :], oml[:, h:h + 1], lb[:, h:h + 1], ALU.mult, ALU.add).then_inc(s_decay, 1)
                dve.wait_ge(s_decay, h + 1)
                if h:
                    dve.wait_ge(s_w, 9 * h)
                own.tick(dve.tensor_scalar(hk[:, :], hf[:, :], -1.0, 1.0, ALU.mult, ALU.add))
                dve.wait_ge(s_ln, h + 1)
                own.wait()
                dve.tensor_tensor_scan(hf[:, :], reset[:, :], hb[:, :], 0.0, ALU.mult, ALU.add).then_inc(s_diff, 1)
                dve.wait_ge(s_diff, 9 * h + 1)

            def ew(h, j):
                n = 9 * h + j
                b, q = hd[h % 2][0], hd[h % 2][1]
                if n:
                    dve.wait_ge(s_w, n)
                if j < 8:
                    d = hD[:, (n + 1) % 2, :]
                    if j == 0:
                        bc = b[:, :].rearrange("p (c t) -> p c t", t=P)
                        dve.tensor_tensor(d.rearrange("p (c t) -> p c t", t=P), bc[:, :, P - 1:P].to_broadcast([P, TT, P]),
                                          bc, ALU.subtract).then_inc(s_diff, 1)
                    else:
                        L = 64 >> (j - 1)
                        bc = b[:, :].rearrange("p (c t) -> p c t", t=2 * L)
                        dve.tensor_tensor(d.rearrange("p (c t) -> p c t", t=2 * L), bc,
                                          bc[:, :, L - 1:L].to_broadcast([P, SEQ // (2 * L), 2 * L]),
                                          ALU.subtract).then_inc(s_diff, 1)
                dve.wait_ge(s_exp, n + 1)
                d = hD[:, n % 2, :]
                if j == 0:
                    bk.wait_emptied(dve, "u", 3 + 4 * h, 1)
                    if h:
                        bk.wait_filled(dve, "o", h - 1, 1)
                    dve.tensor_tensor(hQb[:, :], q[:, :], d, ALU.mult).then_inc(s_w, 1)
                elif j == 1:
                    if h:
                        bk.wait_filled(dve, "gram", h - 1, 7, 1)
                    dve.tensor_tensor(hW[:, 1, :], hk[:, :], d, ALU.mult).then_inc(s_w, 1)
                else:
                    if j == 2 and h:
                        bk.wait_filled(dve, "gram", h - 1, 8, 1)
                    elif j == 3:
                        bk.wait_filled(dve, "kt", h, 1)
                    elif j > 3:
                        bk.wait_filled(dve, "gram", h, j - 2, 1)
                    wl, wu = level_views(hW[:, j % 2, :], j)
                    dl, du = level_views(d, j)
                    kl, _ = level_views(hk[:, :], j)
                    _, qu = level_views(q[:, :], j)
                    dve.tensor_tensor(wl, kl, dl, ALU.mult)
                    dve.tensor_tensor(wu, qu, du, ALU.mult).then_inc(s_w, 1)

            def us(h):
                if h:
                    bk.wait_filled(dve, "o", h - 1, 1)
                for b in range(2):
                    ps = bk.wait_filled(dve, "us", h, b)
                    for j in range(4 - b):
                        cc = 4 * b + j
                        u = ps[:, j * P:(j + 1) * P]
                        ins = (dve.scalar_tensor_tensor(hS[:, cc + 1, :], hS[:, cc, :], heb[:, cc:cc + 1], u, ALU.mult, ALU.add)
                               if cc else dve.tensor_copy(hS[:, 1, :], u))
                        if j == 3 - b:
                            bk.empty(ins, "us", h, b)
                            bk.wait_emptied(dve, "us", h, b)
                        else:
                            own.seq(ins)
                dve.sem_inc(s_state, 1)

            def gram(h, j):
                if h and j == 2:
                    bk.wait_filled(dve, "o", h - 1, 1)
                for b in range(2):
                    ps = bk.wait_filled(dve, "gram", h, j, b)
                    if j > 2:
                        bk.wait_emptied(dve, "gram", h, j - 1, b)
                    m = hgm[:, j - 2:j - 1, :].to_broadcast([P, 4, P])
                    bk.empty(dve.copy_predicated(hAT[:, b, :, :], m, ps[:, :].rearrange("p (a n) -> p a n", n=P)),
                             "gram", h, j, b)

            def o(h):
                gate = hd[h % 2][3]
                for i in range(2):
                    bk.wait_emptied(dve, "u", 5 + 4 * h, i)
                own.tick(dve.tensor_scalar(gate[:, 0:SEQ], gate[:, 0:SEQ], cols[:, 48 + h:49 + h], None, ALU.mult))
                for b in range(2):
                    dve.wait_ge(s_rs, 2 * h + b + 1)
                    own.seq(dve.tensor_tensor(ho[:, b, :], ho[:, b, :], ho2[:, b, :], ALU.mult))
                    t = slice(512 * b, 512 * b + 512)
                    dve.tensor_tensor(mix_h[:, h, t], ho[:, b, :], gate[:, t], ALU.mult).then_inc(s_y, 1)

            do = {"unit": unit, "pos": pos, "gelu": gelu, "ckv": ckv, "prep": prep, "ew": ew, "us": us, "gram": gram, "o": o}
            for step in order:
                if step[0] in do:
                    do[step[0]](*step[1:])

    NIT = 2 * TT
    blocks = []
    for it in range(NIT):
        qt = it // 2
        blocks.append([(0, 0)] + [(1, j) for j in range(qt + 1)] + [(2, j) for j in range(max(0, qt - 4), qt + 1)])
    first = [sum(len(b) for b in blocks[:it]) for it in range(NIT)]

    def chunks(it, br):
        qt = it // 2
        lo, hi = (0 if br == 1 else max(0, qt - 4)) * P, (qt + 1) * P
        return [(a, min(a + 512, hi)) for a in range(lo, hi, 512)]

    at_bk = Banks(nc, psum, "at")
    OUT_BANK = (4, 5)
    s_ot = sem("outputs_copied")
    ADA2 = [(v, half) for v in (2, 4, 3, 5) for half in range(2)]

    def tickets(it):
        t = []
        for br in (1, 2):
            for i, (a, b) in enumerate(chunks(it, br)):
                n = {128: 4, 256: 2}.get(b - a, 1)
                t += [(h0, n, br, i, a, b) for h0 in range(0, HG, n)]
        return t + [None]

    flat = [(it, b) for it in range(NIT) for b in range(len(blocks[it]))]
    steps = [("keys", 0), ("keys", 1), ("qprep", 0), ("p1", 0, 0), ("p1", 0, 1), ("low", 0), ("low", 1), ("p1", 0, 2),
             ("maxend", 0), ("keys", 2), ("keys", 3), ("qprep", 1), ("low", 2), ("low", 3), ("p1", 1, 0), ("p1", 1, 1), ("values",), ("p1", 1, 2), ("maxend", 1), ("qprep", 2)]
    assert len(tickets(0)) == len(tickets(1)) == 3
    steps += [("m4", 0), ("qaug", 0), ("m4", 1), ("qaug", 1), ("S", 0, 0), ("S", 0, 1)]
    late = []
    for v in range(len(ADA2)):
        late += [[("acc2", v, k)] for k in range(KT)]
        if v:
            late[-KT] = [("ada2", v - 1), ("ada2_out", v - 1)] + late[-KT]
    late.append([("ada2", len(ADA2) - 1), ("ada2_out", len(ADA2) - 1)])
    ended = []
    for n0 in range(0, len(flat), 2):
        pair = [(n,) + flat[n] for n in (n0, n0 + 1)]
        if pair[0][2] == 0 and 2 <= pair[0][1] + 1 < NIT:
            steps += [("m4", pair[0][1] + 1), ("qaug", pair[0][1] + 1)]
        between = []
        for n, it, b in pair:
            if it + 2 < NIT:
                k, nb = len(tickets(it + 2)), max(2, len(blocks[it]) - 4)
                if b:
                    between += [("p1", it + 2, i) for i in range(min(k, k * (b - 1) // nb), min(k, k * b // nb))]
                if b == nb:
                    between.append(("maxend", it + 2))
                if b == max(1, len(blocks[it]) - 3) and it + 3 < NIT:
                    between.append(("qprep", it + 3))
        for n, it, b in pair:
            if n + 2 < len(flat):
                steps.append(("S",) + flat[n + 2])
                steps += between[:1]
                between = between[1:]
        before, ended = ended, []
        for n, it, b in pair:
            if n == n0 + 1 and b == 0 and 2 <= it + 1 < NIT:
                steps += between + [("m4", it + 1), ("qaug", it + 1)]
                between = []
            steps.append(("pv", it, b))
            steps += between[:1]
            between = between[1:]
            steps += [(kind,) + m[1:] for m in before if m[0] == n - 2 for kind in ("token_major", "combine")]
            if n == n0:
                steps += between[:1]
                between = between[1:]
            else:
                steps += between
            if b == len(blocks[it]) - 1 or blocks[it][b + 1][0] != blocks[it][b][0]:
                steps.append(("copy_out", it, blocks[it][b][0]))
                ended.append((n, it, blocks[it][b][0]))
            if b == 2 and it:
                steps += [("yt", it - 1)]
            if n >= 8 and n % 2 == 0 and (n - 8) // 2 < len(late):
                steps += late[(n - 8) // 2]
    steps += [(kind,) + m[1:] for m in ended for kind in ("token_major", "combine")]
    steps.append(("yt", NIT - 1))
    assert (len(flat) - 8) // 2 >= len(late)
    for step in steps:
        if step[0] == "p1":
            at_bk.plan((0, 1), *step)
        elif step[0] == "S":
            at_bk.plan((2, 3), *step)
        elif step[0] == "token_major":
            at_bk.plan((6,), *step)
        elif step[0] in ("m4", "yt", "ada2"):
            at_bk.plan((7,), *step)

    s_rows, s_kb, s_kp = sem("positions_ready"), sem("keys_low_ready"), sem("keys_high_ready")
    s_kst_a = sem("first_keys_laid_out")
    s_ka, s_slope = sem("keys_doubled"), sem("slopes_ready")
    s_va, s_gates = sem("values_ready"), sem("gates_ready")
    s_q, s_negm, s_qaug = sem("queries_split"), sem("maxima_ready"), sem("maxima_in_queries")
    s_pv, s_ytok = sem("probs_used"), sem("y_nsa_ready")
    s_wa2 = [sem("ada2_loaded0"), sem("ada2_loaded1")]
    s_acc2, s_half, s_brow = sem("ada2_summed"), sem("ada2_half_used"), sem("brow_loaded")
    s_wo = [sem("wo_loaded0"), sem("wo_loaded1")]
    wov = w_out[0].rearrange("(k p) n -> p k n", p=P)
    ch3 = {e: sem(f"{e}_chain_c") for e in ("act", "dve", "pool")}
    vw = hd[0][3][:, :].rearrange("p (a n) -> p a n", n=UW)

    with nc.Block() as block:
        @block.sync
        def _(sp):
            sp.dma_start(brow[:, 0:DM], b_ada[:, 2 * DM:3 * DM]).then_inc(s_brow, 16)
            sp.dma_start(brow[:, DM:2 * DM], b_ada[:, 5 * DM:6 * DM]).then_inc(s_brow, 16)
            for w in range(2 * len(ADA2)):
                vec, half = ADA2[w // 2]
                if w >= 2:
                    sp.wait_ge(s_half, w - 1)
                at, k = vec * DM + half * 512, (w % 2) * (KT // 2)
                sp.dma_start(wa2[:, w % 2, :, :], wada_v[:, k:k + KT // 2, at:at + 512]).then_inc(s_wa2[w % 2], 16)
                if w == 1:
                    sp.wait_ge(s_kp, 2 * GROUPS)
                    sp.wait_ge(s_va, 5)
                    sp.wait_ge(s_gates, 1)
                    for u in range(2):
                        sp.dma_start(wo_raw[:, u, :, :], wov[:, :, 256 * u:256 * u + 256]).then_inc(s_wo[u], 16)

        @block.gpsimd
        def _(pool):
            own = Chain(pool, ch3["pool"])
            pool.iota(kst[1][64:71, :], [[1, SEQ]], base=0, channel_multiplier=0,
                      allow_small_or_imprecise_dtypes=True).then_inc(s_rows, 1)
            for g in range(GROUPS):
                for hh in range(HG):
                    pool.memset(mix_n[64:65, g, hh * P:(hh + 1) * P], SLOPES[4 * g + hh]).then_inc(s_slope, 1)
            pool.wait_ge(s_rows, 1)
            pool.wait_ge(s_slope, 2 * HG)
            for g in range(GROUPS):
                for hh in range(HG):
                    own.tick(pool.memset(negm[:, g, hh, 0:1], SLOPES[4 * g + hh]))
            own.tick(pool.memset(va[:, :, :, :, DH:DH + 1], 1.0))

        @block.tensor
        def _(pe):
            def p1(it, n):
                qt, g = divmod(it, 2)
                s = it % 4
                if n == 0:
                    pe.wait_ge(s_q, it + 1)
                    pe.wait_ge(s_kp, 2 * g + 2)
                ps = at_bk.begin(pe, "p1", it, n)
                if tickets(it)[n] is None:
                    for hh in range(HG):
                        o = ps[:, hh * 64:(hh + 1) * 64]
                        pe.matmul(o, q_a[:, s, hh * P:(hh + 1) * P], kc_a[:, g, :], start=True, stop=False,
                                  skip_group_check=True)
                        pe.matmul(o, q_b[0:65, s, hh * P:(hh + 1) * P], kc_b[0:65, g, :], start=False, stop=False,
                                  skip_group_check=True)
                        last = pe.matmul(o, ident_bf[:, :], cmp_q[:, qt, :], start=False, stop=True, skip_group_check=True)
                else:
                    h0, heads, br, i, a, b = tickets(it)[n]
                    masks = [(qt, causal_q)] + ([(qt - 4, edge_q)] if br == 2 and qt >= 4 else [])
                    masks = [(j, m) for j, m in masks if a <= j * P < b]
                    for hh in range(heads):
                        at = hh * (b - a)
                        last = pe.matmul(ps[:, at:at + b - a], q_b[0:65, s, (h0 + hh) * P:(h0 + hh + 1) * P],
                                         kp[:, br - 1, g, a:b], start=True, stop=not masks, skip_group_check=True)
                        for j, m in masks:
                            last = pe.matmul(ps[:, at + j * P - a:at + j * P - a + P], ident_bf[:, :], m[:, :], start=False,
                                             stop=j == masks[-1][0], skip_group_check=True)
                at_bk.fill(last, "p1", it, n)

            def m4(it):
                pe.wait_ge(s_negm, it + 1)
                ps = at_bk.begin(pe, "m4", it)
                for hh in range(HG):
                    last = pe.matmul(ps[64:71, hh * P:(hh + 1) * P], negm[:, it % 2, hh, :], ident[:, :], start=True, stop=True)
                at_bk.fill(last, "m4", it)

            def S(it, b):
                qt, g = divmod(it, 2)
                br, j = blocks[it][b]
                s = it % 4
                if b == 0:
                    pe.wait_ge(s_qaug, it + 1)
                elif b == 1:
                    pe.wait_ge(s_kb, 2 * g + 2)
                    pe.wait_ge(s_ka, 2 * g + 2)
                ps = at_bk.begin(pe, "S", it, b)
                if br == 0:
                    o, k_a, k_b = ps[0:64, :], kc_a[:, g, :], kc_b[:, g, :]
                    masks = [cmp_k[:, qt * P:(qt + 1) * P]]
                else:
                    keys = slice(j * P, (j + 1) * P)
                    o, k_a, k_b = ps[:, :], ka_a[:, br - 1, g, keys], ka_b[:, br - 1, g, keys]
                    masks = [causal_k[:, :]] * (j == qt) + [edge_k[:, :]] * (br == 2 and j == qt - 4)
                n = o.shape[0]
                pe.matmul(o, k_a, q_a[:, s, :], start=True, stop=False, skip_group_check=True)
                last = pe.matmul(o, k_b, q_b[:, s, :], start=False, stop=not masks, skip_group_check=True)
                for i, m in enumerate(masks):
                    last = pe.matmul(o.rearrange("k (h q) -> k h q", h=HG), ident_bf[0:n, 0:n],
                                     m.unsqueeze(1).to_broadcast([n, HG, P]), start=False, stop=i == len(masks) - 1,
                                     skip_group_check=True)
                at_bk.fill(last, "S", it, b)

            def pv(it, b):
                qt, g = divmod(it, 2)
                br, j = blocks[it][b]
                n, m = first[it] + b, 3 * it + br
                starts = b == 0 or blocks[it][b - 1][0] != br
                if starts and m >= 2:
                    pe.wait_ge(s_ot, m - 1)
                if n == 0:
                    pe.wait_ge(s_va, 5)
                at_bk.wait_emptied(pe, "S", it, b)
                rows = 64 if br == 0 else P
                v = vc_sb[:, g, :] if br == 0 else va[:, br - 1, j, g, :]
                pe.matmul(psum[OUT_BANK[m % 2]][0:DH + 1, :], v, pt[0:rows, n % 4, :], start=starts,
                          stop=b == len(blocks[it]) - 1 or blocks[it][b + 1][0] != br, skip_group_check=True).then_inc(s_pv, 1)

            def token_major(it, br):
                m = 3 * it + br
                pe.wait_ge(s_ot, m + 1)
                ps = at_bk.begin(pe, "token_major", it, br)
                for hh in range(HG):
                    last = pe.transpose(ps[:, hh * 65:(hh + 1) * 65], ot[:, m % 2, hh * P:(hh + 1) * P],
                                        ident[0:DH + 1, 0:DH + 1])
                at_bk.fill(last, "token_major", it, br)

            def yt(it):
                pe.wait_ge(s_ytok, it + 1)
                ps = at_bk.begin(pe, "yt", it)
                for j in range(2):
                    last = pe.transpose(ps[:, j * P:(j + 1) * P], yb[:, it % 2, 0, j * P:(j + 1) * P], ident[:, :])
                at_bk.fill(last, "yt", it)

            def ada2(v):
                vec, half = ADA2[v]
                pe.wait_ge(s_acc2, v + 1)
                ps = at_bk.begin(pe, "ada2", v)
                if vec in (3, 4):
                    for j in range(4):
                        last = pe.matmul(ps[:, j:j + 1], acc2[:, j * P:(j + 1) * P], ones[:, 0:1], start=True, stop=True)
                else:
                    at = (vec == 5) * DM + half * 512
                    pe.wait_ge(s_brow, 32)
                    pe.matmul(ps[:, :], ones[:, :], acc2[:, :], start=True, stop=False)
                    last = pe.matmul(ps[:, :], ones[0:1, :], brow[:, at:at + 512], start=False, stop=True)
                at_bk.fill(last, "ada2", v)

            do = {"p1": p1, "m4": m4, "S": S, "pv": pv, "token_major": token_major, "yt": yt, "ada2": ada2}
            for step in steps:
                if step[0] in do:
                    do[step[0]](*step[1:])

        @block.scalar
        def _(act):
            def mix(it):
                qt, g = divmod(it, 2)
                ps = at_bk.wait_filled(act, "yt", it)
                at_bk.empty(act.activation(mix_n[:, 2 * g:2 * g + 2, qt * P:(qt + 1) * P],
                                           ps[:, 0:2 * P].rearrange("p (j t) -> p j t", j=2), ACT.Copy), "yt", it)

            for br in range(2):
                act.activation(kst[br][0:DH, :], hd[0][br][0:DH, :], ACT.Copy).then_inc(s_kst_a, 1)
            act.activation(gates[:, :, :], vw[:, :, P:UW], ACT.Sigmoid).then_inc(s_gates, 1)
            def weights(it, b):
                n = first[it] + b
                ps = at_bk.wait_filled(act, "S", it, b)
                if n >= 4:
                    act.wait_ge(s_pv, n - 3)
                rows = 64 if blocks[it][b][0] == 0 else P
                at_bk.empty(act.activation(pt[0:rows, n % 4, :], ps[0:rows, :], ACT.Exp), "S", it, b)

            def keys(n):
                g, br = divmod(n, 2)
                act.wait_ge(s_kp, n + 1)
                act.activation(ka_b[64:71, br, g, :], kst[br][64:71, :], ACT.Copy).then_inc(ch3["act"], 1)
                act.activation(ka_a[0:64, br, g, :], kp[0:64, br, g, :].bitcast(F32), ACT.Copy).then_inc(ch3["act"], 1)
                act.activation(ka_a[64:128, br, g, :], kp[0:64, br, g, :].bitcast(F32), ACT.Copy).then_inc(s_ka, 1)

            def copy_out(it, br):
                m = 3 * it + br
                act.wait_ge(s_pv, first[it] + 1 + max(b for b in range(len(blocks[it])) if blocks[it][b][0] == br))
                if m >= 2:
                    at_bk.wait_filled(act, "token_major", *divmod(m - 2, 3))
                act.activation(ot[:, m % 2, :], psum[OUT_BANK[m % 2]][0:DH + 1, :], ACT.Copy).then_inc(s_ot, 1)

            do = {"keys": keys, "S": weights, "yt": mix, "copy_out": copy_out}
            for step in steps:
                if step[0] in do:
                    do[step[0]](*step[1:])

        @block.vector
        def _(dve):
            own = Chain(dve, ch3["dve"])

            def keys(n):
                g, br = divmod(n, 2)
                if n < 2:
                    dve.wait_ge(s_rows, 1)
                    own.tick(dve.tensor_scalar(kst[br][64:71, :], kst[1][64:71, :], row_of[64:71, 0:1],
                                               row_of[64:71, 1 + br:2 + br], ALU.mult, ALU.add))
                if g:
                    own.seq(dve.tensor_copy(kst[br][0:DH, :], hd[0][br][g * DH:(g + 1) * DH, :]))
                else:
                    dve.wait_ge(s_kst_a, br + 1)
                    own.wait()
                dve.tensor_copy(kp[:, br, g, :], kst[br][0:65, :]).then_inc(s_kp, 1)

            def low(n):
                g, br = divmod(n, 2)
                dve.wait_ge(s_kp, n + 1)
                dve.tensor_tensor(ka_b[0:64, br, g, :], kst[br][0:64, :], kp[0:64, br, g, :].bitcast(F32),
                                  ALU.subtract).then_inc(s_kb, 1)
                dve.wait_ge(s_kb, n + 1)

            def qprep(it):
                qt, g = divmod(it, 2)
                s = it % 4
                tok = slice(qt * P, (qt + 1) * P)
                own.wait()
                for par in range(2):
                    own.tick(dve.tensor_scalar(qst[:, par::2, :], nq[par * DH:(par + 1) * DH, 2 * g:2 * g + 2, tok],
                                               DH ** -0.5, None, ALU.mult))
                own.wait()
                if it >= 4:
                    at_bk.wait_filled(dve, "S", it - 4, len(blocks[it - 4]) - 1)
                q = qst[:, :, :].rearrange("p h t -> p (h t)")
                if it < 4:
                    dve.wait_ge(s_slope, 2 * HG)
                    own.tick(dve.tensor_copy(q_b[64:65, s, :], mix_n[64:65, g, 0:HG * P]))
                own.seq(dve.tensor_copy(q_a[0:64, s, :], q))
                own.tick(dve.tensor_copy(q_b[0:64, s, :], q_a[0:64, s, :].bitcast(F32)))
                own.tick(dve.tensor_tensor(q_a[64:128, s, :], q, q_a[0:64, s, :].bitcast(F32), ALU.subtract))
                own.wait()
                dve.sem_inc(s_q, 1)

            def values():
                for br in range(2):
                    src = (hd[0][2][:, :, :] if br == 0 else vw[:, :, 0:P]).rearrange("p t (g d) -> p t g d", g=GROUPS)
                    for g in range(GROUPS):
                        dve.tensor_copy(va[:, br, :, g, 0:DH], src[:, :, g, :]).then_inc(s_va, 1)
                dve.wait_ge(ch3["pool"], 8 + 1)
                dve.sem_inc(s_va, 1)

            def maxima(it, n):
                ps = at_bk.wait_filled(dve, "p1", it, n)
                if tickets(it)[n] is None:
                    x, o, neg = ps[:, 0:HG * 64].rearrange("p (h n) -> p h n", h=HG), mx[:, :, 0:1], True
                else:
                    h0, heads, br, i, a, b = tickets(it)[n]
                    x = ps[:, 0:heads * (b - a)].rearrange("p (h n) -> p h n", h=heads)
                    o, neg = pm[:, h0:h0 + heads, 2 * (br - 1) + i:2 * (br - 1) + i + 1], False
                at_bk.empty(dve.tensor_reduce(o, x, axis=AX.X, op=ALU.max, negate=neg), "p1", it, n)

            def maxend(it):
                g = it % 2
                for n in (-1, -2):
                    at_bk.wait_emptied(dve, "p1", it, len(tickets(it)) + n)
                own.tick(dve.tensor_scalar(mx[:, :, 0:1], mx[:, :, 0:1], FLOOR, None, ALU.min))
                for br in (1, 2):
                    n = len(chunks(it, br))
                    own.tick(dve.tensor_reduce(mx[:, :, br:br + 1], pm[:, :, 2 * (br - 1):2 * (br - 1) + n], axis=AX.X,
                                               op=ALU.max, negate=True))
                own.wait()
                if it >= 2:
                    at_bk.wait_filled(dve, "m4", it - 2)
                else:
                    dve.wait_ge(ch3["pool"], 8)
                own.seq(dve.tensor_copy(negm[:, g, :, 1:4].bitcast(F32R), mx[:, :, :]))
                own.tick(dve.tensor_tensor(negm[:, g, :, 4:7], mx[:, :, :], negm[:, g, :, 1:4], ALU.subtract))
                own.wait()
                dve.sem_inc(s_negm, 1)

            def qaug(it):
                ps = at_bk.wait_filled(dve, "m4", it)
                at_bk.empty(dve.tensor_copy(q_b[64:71, it % 4, :], ps[64:71, :]), "m4", it)
                at_bk.wait_emptied(dve, "m4", it)
                dve.sem_inc(s_qaug, 1)

            def combine(it, br):
                qt, g = divmod(it, 2)
                y = yb[:, it % 2, :, :]
                if it >= 2 and br == 0:
                    at_bk.wait_filled(dve, "yt", it - 2)
                if it == 0 and br == 0:
                    dve.wait_ge(s_gates, 1)
                ps = at_bk.wait_filled(dve, "token_major", it, br)
                o = ps[:, 0:HG * 65].rearrange("p (h n) -> p h n", h=HG)
                r = rc[:, br, :]
                own.seq(dve.tensor_scalar(r, o[:, :, DH:DH + 1].rearrange("p h n -> p (h n)"), 1e-30, None, ALU.max))
                own.seq(dve.reciprocal(r, r))
                gt = gates[:, qt, :].rearrange("p (h b) -> p b h", b=3)[:, br, HG * g:HG * g + HG]
                own.seq(dve.tensor_tensor(r, r, gt, ALU.mult))
                at_bk.empty(dve.tensor_tensor(y[:, min(br, 1), :].rearrange("p (h n) -> p h n", h=HG), o[:, :, 0:DH],
                                              r.unsqueeze(2).to_broadcast([P, HG, DH]), ALU.mult), "token_major", it, br)
                at_bk.wait_emptied(dve, "token_major", it, br)
                if br == 1:
                    own.seq(dve.tensor_tensor(y[:, 0, :], y[:, 0, :], y[:, 1, :], ALU.add))
                elif br == 2:
                    dve.tensor_tensor(y[:, 0, :], y[:, 0, :], y[:, 1, :], ALU.add).then_inc(s_ytok, 1)

            def acc2_step(v, k):
                kh, kk = divmod(k, KT // 2)
                if kk == 0:
                    dve.wait_ge(s_wa2[kh], 16 * (v + 1))
                if k == 0:
                    if v:
                        at_bk.wait_filled(dve, "ada2", v - 1)
                    own.tick(dve.tensor_scalar(acc2[:, :], wa2[:, 0, 0, :], silu_c[:, 0:1], None, ALU.mult))
                    return
                own.wait()
                i = dve.scalar_tensor_tensor(acc2[:, :], wa2[:, kh, kk, :], silu_c[:, k:k + 1], acc2[:, :], ALU.mult, ALU.add)
                if kk < KT // 2 - 1:
                    own.tick(i)
                    return
                i.then_inc(s_half, 1)
                dve.wait_ge(s_half, 2 * v + kh + 1)
                if kh:
                    dve.sem_inc(s_acc2, 1)

            def ada2_out(v):
                vec, half = ADA2[v]
                ps = at_bk.wait_filled(dve, "ada2", v)
                if vec in (3, 4):
                    j = slice(4 * half, 4 * half + 4)
                    ins = dve.scalar_tensor_tensor(ada[:, vec - 1, j], ps[:, 0:4], 1.0 if vec == 4 else 0.0,
                                                   cols[:, 8 * vec + 4 * half:8 * vec + 4 * half + 4], ALU.add, ALU.add)
                else:
                    ins = dve.tensor_copy((gate1 if vec == 2 else gate2)[:, 512 * half:512 * half + 512], ps[:, :])
                at_bk.empty(ins, "ada2", v)

            do = {"keys": keys, "low": low, "values": values, "qprep": qprep, "p1": maxima, "maxend": maxend, "qaug": qaug, "combine": combine,
                  "acc2": acc2_step, "ada2_out": ada2_out}
            for step in steps:
                if step[0] in do:
                    do[step[0]](*step[1:])

    wo_bk = Banks(nc, psum, "wo")
    for u in range(4):
        for pr in range(4):
            wo_bk.plan(tuple(range(8)), u, pr)
    s_x1 = sem("x_reloaded")
    s_wohi, s_wolo = sem("wo_hi_ready"), sem("wo_lo_ready")
    s_mhi, s_mlo = sem("mix_hi_ready"), sem("mix_lo_ready")
    s_mv, s_ln, s_rstd, s_xn = sem("moments_ready"), sem("ln_ready"), sem("rstd_ready"), sem("normalized")
    s_fraw, s_lnp = [sem("fw_loaded0"), sem("fw_loaded1")], sem("ln_rows_loaded")
    ch4 = {e: sem(f"{e}_chain_d") for e in ("act", "dve", "pool")}

    w1v = ffn_w1[0].rearrange("(k p) n -> p k n", p=P)
    w3v = ffn_w3[0].rearrange("(k p) n -> p k n", p=P)

    def kcols(t):
        return t.rearrange("p (k n) -> p k n", n=P)

    def mix_src(k):
        return mix_h[:, k, :] if k < HG else mix_n[:, k - HG, :]

    with nc.Block() as block:
        @block.sync
        def _(sp):
            sp.dma_start(x1[:, :, :], x[0].rearrange("(t p) d -> p t d", p=P)).then_inc(s_x1, 16)
            for u in range(2, 4):
                sp.wait_ge(s_wolo, u - 1)
                sp.dma_start(wo_raw[:, u % 2, :, :], wov[:, :, 256 * u:256 * u + 256]).then_inc(s_wo[u % 2], 16)
            sp.wait_ge(s_mlo, HG)
            sp.dma_start(kcols(fw_raw[:, 0, :]), w1v[:, :, 0:P]).then_inc(s_fraw[0], 16)
            sp.dma_start(kcols(fw_raw[:, 1, :]), w3v[:, :, 0:P]).then_inc(s_fraw[1], 16)
            sp.dma_start(ln1g[:, :], ln1_g.to_broadcast([P, DM])).then_inc(s_lnp, 16)
            sp.dma_start(ln1b[:, :], ln1_b.to_broadcast([P, DM])).then_inc(s_lnp, 16)

        @block.gpsimd
        def _(pool):
            pool.wait_ge(s_wolo, 1)
            for u in range(1, 4):
                pool.wait_ge(s_wohi, u + 1)
                pool.tensor_tensor(wo_lo[:, u % 2, :, :], wo_raw[:, u % 2, :, :], wo_hi[:, u % 2, :, :].bitcast(F32),
                                   ALU.subtract).then_inc(s_wolo, 1)

        @block.tensor
        def _(pe):
            for u in range(4):
                pe.wait_ge(s_wolo, u + 1)
                for pr in range(4):
                    ps = wo_bk.begin(pe, u, pr)
                    for j in range(2):
                        tok = slice((2 * pr + j) * P, (2 * pr + j + 1) * P)
                        for k in range(KT):
                            if u == 0 and pr == 0 and j == 0:
                                pe.wait_ge(s_mlo, k + 1)
                            last = split3(pe, ps[:, 256 * j:256 * j + 256], mix_hi[:, k, tok], mix_lo[:, k, tok],
                                          wo_hi[:, u % 2, k, :], wo_lo[:, u % 2, k, :], k == 0, k == KT - 1)
                    wo_bk.fill(last, u, pr)

        @block.scalar
        def _(act):
            def take(u):
                act.wait_ge(s_wo[u % 2], 16 * (u // 2 + 1))
                if u >= 2:
                    wo_bk.wait_filled(act, u - 2, 3)
                act.activation(wo_hi[:, u % 2, :, :], wo_raw[:, u % 2, :, :], ACT.Copy).then_inc(s_wohi, 1)

            for k in range(KT):
                if k == 0:
                    take(0)
                act.activation(mix_hi[:, k, :], mix_src(k), ACT.Copy).then_inc(s_mhi, 1)
            for u in range(1, 4):
                take(u)
            for pr in range(4):
                act.wait_ge(s_mv, pr + 1)
                t = slice(2 * pr, 2 * pr + 2)
                act.activation(rstd[:, t, 0:1], mv[:, t, 1:2], ACT.Ln, bias=eps[:, 0:1]).then_inc(s_ln, 1)
                act.wait_ge(s_ln, 2 * pr + 1)
                act.activation(rstd[:, t, 0:1], rstd[:, t, 0:1], ACT.Exp, scale=-0.5).then_inc(s_ln, 1)
                act.wait_ge(s_rstd, pr + 1)
                for j in range(2):
                    i = 2 * pr + j
                    act.activation(x1[:, i, :], x1[:, i, :], ACT.Identity, scale=rstd[:, i, 0:1], bias=rstd[:, i, 1:2])\
                       .then_inc(s_xn, 1)

        @block.vector
        def _(dve):
            own = Chain(dve, ch4["dve"])

            def nmr(pr):
                t = slice(2 * pr, 2 * pr + 2)
                dve.wait_ge(s_ln, 2 * pr + 2)
                dve.scalar_tensor_tensor(rstd[:, t, 1:2], mv[:, t, 0:1], -1.0, rstd[:, t, 0:1], ALU.mult, ALU.mult)\
                   .then_inc(s_rstd, 1)

            dve.wait_ge(s_wohi, 1)
            dve.tensor_tensor(wo_lo[:, 0, :, :], wo_raw[:, 0, :, :], wo_hi[:, 0, :, :].bitcast(F32), ALU.subtract)\
               .then_inc(s_wolo, 1)
            for k in range(KT):
                dve.wait_ge(s_mhi, k + 1)
                dve.tensor_tensor(mix_lo[:, k, :], mix_src(k), mix_hi[:, k, :].bitcast(F32), ALU.subtract).then_inc(s_mlo, 1)
            own.tick(dve.tensor_tensor(hcol[:, 0, :], cols[:, 92:100], ada[:, 3, :], ALU.mult))
            own.seq(dve.tensor_tensor(hcol[:, 1, :], cols[:, 100:108], ada[:, 3, :], ALU.mult))
            own.tick(dve.tensor_tensor(hcol[:, 1, :], hcol[:, 1, :], ada[:, 2, :], ALU.add))
            dve.wait_ge(s_x1, 16)
            for u in range(4):
                cs = slice(256 * u, 256 * u + 256)
                for pr in range(4):
                    ps = wo_bk.wait_filled(dve, u, pr)
                    n = 4 * u + pr
                    if n >= 2:
                        own.wait()
                    t = wt[:, n % 2, :].rearrange("p (a n) -> p a n", a=2)
                    wo_bk.empty(dve.tensor_tensor(t, ps[:, :].rearrange("p (a n) -> p a n", a=2),
                                                  gate1[:, cs].unsqueeze(1).to_broadcast([P, 2, 256]), ALU.mult), u, pr)
                    wo_bk.wait_emptied(dve, u, pr)
                    xs = x1[:, 2 * pr:2 * pr + 2, cs]
                    own.tick(dve.scalar_tensor_tensor(xs, xs, ALPHA, t, ALU.mult, ALU.add))
                    if u == 3:
                        own.wait()
                        for j in range(2):
                            i = 2 * pr + j
                            for q in range(2):
                                own.tick(dve.bn_stats(stat[:, j, 6 * q:6 * q + 6], x1[:, i, 512 * q:512 * q + 512]))
                            own.wait()
                            ins = dve.bn_aggr(mv[:, i, :], stat[:, j, :])
                            if j == 0:
                                own.tick(ins)
                        ins.then_inc(s_mv, 1)
                        if pr:
                            nmr(pr - 1)
            nmr(3)

    NUP, NUNITS = 2 * NFF, 3 * NFF
    s_fhi = sem("fw_hi_ready")
    s_flo = sem("fw_lo_ready_plus_2")
    s_fused = sem("fw_units_used_plus_2")
    s_silu2, s_prod, s_ffhi = sem("silu_ready"), sem("product_ready"), sem("ff_hi_ready")
    s_ff = sem("ff_tiles_ready_plus_2")
    s_tr, s_tre, s_h2 = sem("h2_transposed"), sem("h2_turned_read"), sem("h2_split")
    s_dn = sem("down_banks_read")
    s_mv2, s_ln2, s_rstd2, s_xn2 = sem("moments2_ready"), sem("ln2_ready"), sem("rstd2_ready"), sem("normalized2")
    s_fin_pool = sem("rows_ready_by_gpsimd")
    s_lnp2, s_res, s_fin = sem("ln2_rows_loaded"), sem("residual_ready"), sem("rows_ready")
    ch5 = {e: sem(f"{e}_chain_e") for e in ("act", "dve", "pool")}

    with nc.Block() as block:
        @block.sync
        def _(sp):
            def load(slot, src, after):
                sp.wait_ge(s_flo, after)
                sp.dma_start(kcols(fw_raw[:, slot, :]) if len(src.shape) == 3 else fw_raw[:, slot, :], src)\
                  .then_inc(s_fraw[slot], 16)
            for half in range(2):
                u0 = half * NUNITS
                with sp.Fori(1 - half, NFF) as f:
                    load(0, w1v[:, :, bass.ds(f * P, P)], u0 + 1 + 2 * f)
                    load(1, w3v[:, :, bass.ds(f * P, P)], u0 + 2 + 2 * f)
                with sp.Fori(0, NFF // 2) as k:
                    for j in range(2):
                        load(j, ffn_w2[0, bass.ds(k * 2 * P + j * P, P), :], u0 + NUP + 1 + j + 2 * k)
            for t in range(TT):
                if t in (4, 5):
                    sp.wait_ge(s_fin_pool, t - 3)
                else:
                    sp.wait_ge(s_fin, t + 1 - 2 * (t > 5))
                sp.dma_start(out[0, t * P:(t + 1) * P, :], x1[:, t, :]).then_inc(s_out, 16)
            sp.wait_ge(s_out, 16 * TT)

        @block.gpsimd
        def _(pool):
            pool.sem_inc(s_flo, 2)

            def low(slot, after):
                pool.wait_ge(s_fhi, after)
                pool.tensor_tensor(fw_lo[:, slot, :], fw_raw[:, slot, :], fw_hi[:, slot, :].bitcast(F32), ALU.subtract)\
                    .then_inc(s_flo, 1)

            for half in range(2):
                u0 = half * NUNITS
                with pool.Fori(0, NFF) as f:
                    low(0, u0 + 1 + 2 * f)
                    low(1, u0 + 2 + 2 * f)
                with pool.Fori(0, NFF // 2) as k:
                    low(0, u0 + NUP + 1 + 2 * k)
                    low(1, u0 + NUP + 2 + 2 * k)
            pool.wait_ge(s_lnp2, 32)
            for n, i in enumerate((4, 5)):
                pool.wait_ge(s_xn2, i + 1)
                pool.tensor_tensor(x1[:, i, :], x1[:, i, :], ln1g[:, :], ALU.mult).then_inc(ch5["pool"], 1)
                pool.wait_ge(ch5["pool"], n + 1)
                pool.tensor_tensor(x1[:, i, :], x1[:, i, :], ln1b[:, :], ALU.add).then_inc(s_fin_pool, 1)

        @block.tensor
        def _(pe):
            pe.sem_inc(s_fused, 2)

            def turn(half):
                for m in range(KT):
                    if m >= 4 or half:
                        pe.wait_ge(s_tre, KT * half + m - 3)
                    for t in range(4):
                        last = pe.transpose(psum[4 + m % 4][:, t * P:(t + 1) * P], x1[:, 4 * half + t, m * P:(m + 1) * P],
                                            ident[:, :])
                    last.then_inc(s_tr, 1)

            for half in range(2):
                u0 = half * NUNITS
                if half:
                    pe.wait_ge(s_dn, 4)
                else:
                    turn(0)
                pe.wait_ge(s_h2, KT * (half + 1))
                with pe.Fori(0, NFF // 2) as i:
                    for par in range(2):
                        pe.wait_ge(s_ff, NFF * half + 1 + par + 2 * i)
                        for b in range(2):
                            u = 2 * par + b
                            pe.wait_ge(s_flo, u0 + 3 + u + 4 * i)
                            w_h, w_l = kcols(fw_hi[:, b, :]), kcols(fw_lo[:, b, :])
                            for k in range(KT):
                                last = split3(pe, psum[2 * par + b][:, :], w_h[:, k, :], w_l[:, k, :], h2_hi[:, k, :],
                                              h2_lo[:, k, :], k == 0, k == KT - 1)
                            last.then_inc(s_fused, 1)
                if half:
                    pe.wait_ge(s_dn, 8)
                else:
                    turn(1)
                    pe.wait_ge(s_tre, 2 * KT)
                pe.wait_ge(s_ff, NFF * (half + 1) + 2)
                for k in range(NFF):
                    pe.wait_ge(s_flo, u0 + NUP + 3 + k)
                    for t in range(4):
                        for nb in range(2):
                            cs = slice(512 * nb, 512 * nb + 512)
                            last = split3(pe, psum[2 * t + nb][:, :], ff_hi[:, k, t * P:(t + 1) * P],
                                          ff_lo[:, k, t * P:(t + 1) * P], fw_hi[:, k % 2, cs], fw_lo[:, k % 2, cs],
                                          k == 0, k == NFF - 1)
                    last.then_inc(s_fused, 1)

        @block.scalar
        def _(act):
            def take(slot, loaded, used):
                act.wait_ge(s_fraw[slot], loaded)
                act.wait_ge(s_fused, used)
                act.activation(fw_hi[:, slot, :], fw_raw[:, slot, :], ACT.Copy).then_inc(s_fhi, 1)

            def norm(lo, hi, n):
                t = slice(lo, hi)
                act.wait_ge(s_mv2, n + 1)
                act.activation(rstd2[:, t, 0:1], mv2[:, t, 1:2], ACT.Ln, bias=eps[:, 0:1]).then_inc(s_ln2, 1)
                act.wait_ge(s_ln2, 2 * n + 1)
                act.activation(rstd2[:, t, 0:1], rstd2[:, t, 0:1], ACT.Exp, scale=-0.5).then_inc(s_ln2, 1)
                act.wait_ge(s_rstd2, n + 1)
                for i in range(lo, hi):
                    act.activation(x1[:, i, :], x1[:, i, :], ACT.Identity, scale=rstd2[:, i, 0:1], bias=rstd2[:, i, 1:2])\
                       .then_inc(s_xn2, 1)

            def turned(half):
                for m in range(KT):
                    act.wait_ge(s_tr, KT * half + m + 1)
                    if m >= 2 or half:
                        act.wait_ge(s_h2, KT * half + m - 1)
                    if half and m < 2:
                        act.wait_ge(s_ff, NFF + 1 + m)
                    act.activation(ft[:, m % 2, :], psum[4 + m % 4][:, :], ACT.Identity, scale=hcol[:, 0, m:m + 1],
                                   bias=hcol[:, 1, m:m + 1]).then_inc(s_tre, 1)

            for half in range(2):
                u0 = half * NUNITS
                n0 = u0 // 2
                for b in range(2):
                    take(b, 16 * (n0 + 1), u0 + 1 + b)
                if not half:
                    turned(0)
                act.wait_ge(s_h2, KT * (half + 1))
                with act.Fori(0, NFF // 2) as i:
                    for par in range(2):
                        take(0, 16 * (n0 + 2 + par) + 32 * i, u0 + 3 + 2 * par + 4 * i)
                        act.wait_ge(s_ff, NFF * half + 1 + par + 2 * i)
                        act.activation(ft[:, par, :], psum[2 * par][:, :], ACT.Silu).then_inc(s_silu2, 1)
                        take(1, 16 * (n0 + 2 + par) + 32 * i, u0 + 4 + 2 * par + 4 * i)
                if half:
                    act.wait_ge(s_res, TT)
                    act.dma_start(ln1g[:, :], ln2_g.to_broadcast([P, DM])).then_inc(s_lnp2, 16)
                    act.dma_start(ln1b[:, :], ln2_b.to_broadcast([P, DM])).then_inc(s_lnp2, 16)
                else:
                    turned(1)
                for pr, (lo, hi) in enumerate(((1, 3), (3, NFF // 2))):
                    if half:
                        norm(2 * pr, 2 * pr + 2, pr)
                    with act.Fori(lo, hi) as k:
                        for b in range(2):
                            take(b, 16 * (n0 + NFF + 1) + 16 * k, u0 + NUP + 1 + b + 2 * k)
            for t in range(4):
                norm(4 + t, 5 + t, 2 + t)

        @block.vector
        def _(dve):
            dve.sem_inc(s_ff, 2)
            own = Chain(dve, ch5["dve"])

            def down(half):
                dve.wait_ge(s_fused, NUNITS * (half + 1) + 2)
                def gate(n):
                    dve.tensor_tensor(gated[:, n, :], psum[n][:, :], gate2[:, 512 * (n % 2):512 * (n % 2) + 512], ALU.mult)\
                       .then_inc(s_dn, 1)
                if half == 0:
                    for n in range(8):
                        gate(n)
                for t in range(4):
                    i = 4 * half + t
                    if half:
                        gate(2 * t)
                        gate(2 * t + 1)
                    for nb in range(2):
                        cs = slice(512 * nb, 512 * nb + 512)
                        dve.wait_ge(s_dn, 8 * half + 2 * t + nb + 1)
                        own.tick(dve.scalar_tensor_tensor(x1[:, i, cs], x1[:, i, cs], ALPHA, gated[:, 2 * t + nb, :], ALU.mult,
                                                          ALU.add))
                    own.wait()
                    for nb in range(2):
                        own.tick(dve.bn_stats(stat2[:, t % 2, 6 * nb:6 * nb + 6], x1[:, i, 512 * nb:512 * nb + 512]))
                    own.wait()
                    ins = dve.bn_aggr(mv2[:, i, :], stat2[:, t % 2, :])
                    if half:
                        ins.then_inc(s_mv2, 1)
                        dve.wait_ge(s_mv2, 3 + t)
                        if t:
                            nmr(3 + t, 4 + t, 1 + t)
                    elif t % 2:
                        ins.then_inc(s_mv2, 1)
                        dve.wait_ge(s_mv2, t // 2 + 1)
                    else:
                        own.seq(ins)
                if half:
                    nmr(7, 8, 5)

            def nmr(lo, hi, n):
                t = slice(lo, hi)
                dve.wait_ge(s_ln2, 2 * n + 2)
                dve.scalar_tensor_tensor(rstd2[:, t, 1:2], mv2[:, t, 0:1], -1.0, rstd2[:, t, 0:1], ALU.mult, ALU.mult)\
                   .then_inc(s_rstd2, 1)

            def affine(tiles):
                dve.wait_ge(s_lnp2, 32)
                for i in tiles:
                    dve.wait_ge(s_xn2, i + 1)
                    own.seq(dve.tensor_tensor(x1[:, i, :], x1[:, i, :], ln1g[:, :], ALU.mult))
                    dve.tensor_tensor(x1[:, i, :], x1[:, i, :], ln1b[:, :], ALU.add).then_inc(s_fin, 1)

            def turned(half):
                for m in range(KT):
                    dve.wait_ge(s_tre, KT * half + m + 1)
                    own.seq(dve.tensor_copy(h2_hi[:, m, :], ft[:, m % 2, :]))
                    dve.tensor_tensor(h2_lo[:, m, :], ft[:, m % 2, :], h2_hi[:, m, :].bitcast(F32), ALU.subtract).then_inc(s_h2, 1)
                dve.wait_ge(s_lnp, 32)
                for i in range(4 * half, 4 * half + 4):
                    own.seq(dve.tensor_tensor(x1[:, i, :], x1[:, i, :], ln1g[:, :], ALU.mult))
                    dve.tensor_tensor(x1[:, i, :], x1[:, i, :], ln1b[:, :], ALU.add).then_inc(s_res, 1)

            turned(0)
            for half in range(2):
                u0 = half * NUNITS
                if half:
                    down(0)
                dve.wait_ge(s_res, 4 * (half + 1))
                with dve.Fori(0, NFF // 2) as i:
                    for par in range(2):
                        f = 2 * i + par
                        done = NFF * half + 1 + par + 2 * i
                        dve.wait_ge(s_silu2, done)
                        dve.wait_ge(s_fused, u0 + 4 + 2 * par + 4 * i)
                        t = ft[:, par, :]
                        dve.tensor_tensor(t, t, psum[2 * par + 1][:, :], ALU.mult).then_inc(s_prod, 1)
                        dve.wait_ge(s_prod, done)
                        dve.tensor_copy(ff_hi[:, f, :], t).then_inc(s_ffhi, 1)
                        dve.wait_ge(s_ffhi, done)
                        dve.tensor_tensor(ff_lo[:, f, :], t, ff_hi[:, f, :].bitcast(F32), ALU.subtract).then_inc(s_ff, 1)
                if half:
                    nmr(0, 2, 0)
                    nmr(2, 4, 1)
                    affine(range(4))
                else:
                    turned(1)
            down(1)
            affine((6, 7))


_INS = ["x", "c", "w_ada", "b_ada", "w_in", "hg_lb_logits", "hg_norm_g", "cmp_pos_k", "cmp_w1_k", "cmp_w2_k",
        "cmp_pos_v", "cmp_w1_v", "cmp_w2_v", "w_out", "ln1_g", "ln1_b", "ffn_w1", "ffn_w3", "ffn_w2", "ln2_g", "ln2_b"]


def kernel(**inputs):
    import numpy as _np
    import concourse.bacc as _bacc
    from concourse import mybir as _mybir
    from concourse.bass_utils import run_bass_kernel_spmd as _run

    nc = _bacc.Bacc("TRN2", target_bir_lowering=False, num_devices=1)
    arrays, args = {}, []
    for name in _INS:
        a = _np.ascontiguousarray(inputs[name])
        arrays[f"in_{name}_dram"] = a
        args.append(nc.dram_tensor(f"in_{name}_dram", a.shape, _mybir.dt.from_np(a.dtype), kind="ExternalInput").ap())
    args.append(nc.dram_tensor("out_0_dram", (1, SEQ, DM), F32, kind="ExternalOutput").ap())
    program(nc, *args)
    r = _run(nc, [arrays], core_ids=[0])
    return r.results[0]["out_0_dram"]
```
